# Optimizing a Trainium2 kernel written in Bass

```python
import math
import jax, jax.numpy as jnp
from jax import lax
import numpy as np

D_MODEL = 1024
BATCH = 1
SEQ = 512
DEPTH = 2

D_MIX = D_MODEL
D_A = D_MIX // 2
N_HEADS_A = 8
HEAD_DIM_A = D_A // N_HEADS_A
CHUNK = 128
D_B = D_MIX - D_A
N_GROUPS_B = 8
HYENA_ORDER = 2
N_PROJ_B = HYENA_ORDER + 1
SHORT_K = 3
IN_COLS = 2 * D_A + N_PROJ_B * D_B
FILTER_EMB = 33
FILTER_BANDS = (FILTER_EMB - 1) // 2
FILTER_WIDTH = 64
FILTER_OUT_SCALE = 0.1
DECAY_TARGET = 1e-2
FAST_DECAY_PCT = 0.3
SLOW_DECAY_PCT = 1.5
MAX_DECAY = math.log(DECAY_TARGET) / FAST_DECAY_PCT
MIN_DECAY = math.log(DECAY_TARGET) / SLOW_DECAY_PCT
D_FF = 2816
HALF_STEP = 0.5
RMS_EPS = 1e-6
LN_EPS = 1e-5

kernel_name = 'hybrid_gmlp_hyena_macaron_encoder'

def _rms_norm(x, g):
    xf = x.astype(jnp.float32)
    y = xf * lax.rsqrt(jnp.mean(jnp.square(xf), axis=-1, keepdims=True) + RMS_EPS)
    return (y * g.astype(jnp.float32)).astype(x.dtype)

def _layer_norm(x, g, b):
    xf = x.astype(jnp.float32)
    mu = jnp.mean(xf, axis=-1, keepdims=True)
    var = jnp.mean(jnp.square(xf - mu), axis=-1, keepdims=True)
    y = (xf - mu) * lax.rsqrt(var + LN_EPS)
    return (y * g.astype(jnp.float32) + b.astype(jnp.float32)).astype(x.dtype)

def _swiglu(h, w_gate, w_up, w_down):
    return (jax.nn.silu(h @ w_gate) * (h @ w_up)) @ w_down

def _spatial_gating(u, v, ln_g, ln_b, w_s, b_s):
    bsz, seq, _ = v.shape
    vn = _layer_norm(v, ln_g, ln_b).reshape(bsz, seq // CHUNK, CHUNK, N_HEADS_A, HEAD_DIM_A)
    mixed = jnp.einsum('hmc,bnchd->bnmhd', w_s, vn) + b_s.T[:, :, None]
    return u * mixed.reshape(bsz, seq, D_A)

def _short_conv(z, w, b):
    seq = z.shape[1]
    pad = SHORT_K // 2
    zp = jnp.pad(z, ((0, 0), (pad, pad), (0, 0)))
    out = b
    for k in range(SHORT_K):
        out = out + zp[:, k:k + seq] * w[k]
    return out

def _hyena_filter_spectrum(seq, w1, b1, w2, b2, w3, b3, freq, w_o):
    t = jnp.linspace(0.0, 1.0, seq, dtype=jnp.float32)[:, None]
    bands = jnp.linspace(1e-4, FILTER_BANDS - 1, FILTER_BANDS, dtype=jnp.float32)
    ang = (2.0 * math.pi / seq) * jnp.arange(seq, dtype=jnp.float32)[:, None] * bands[None, :]
    z = jnp.concatenate([t, jnp.cos(ang), -jnp.sin(ang)], axis=-1)
    h = jnp.sin(freq * (z @ w1 + b1))
    h = jnp.sin(freq * (h @ w2 + b2))
    h = jnp.sin(freq * (h @ w3 + b3))
    h = (h @ w_o).astype(jnp.float32).reshape(seq, HYENA_ORDER, 2, D_B)
    deltas = jnp.abs(jnp.linspace(MIN_DECAY, MAX_DECAY, D_B, dtype=jnp.float32))
    h = h * jnp.exp(-t * deltas)[:, None, None, :]
    fwd, bwd = h[:, :, 0], h[:, :, 1]
    k = jnp.concatenate([fwd, jnp.zeros_like(fwd[:1]), bwd[:0:-1]], axis=0)
    return jnp.fft.rfft(k, axis=0)

def _long_conv(u, k_f, skip):
    seq = u.shape[1]
    uf32 = u.astype(jnp.float32)
    y = jnp.fft.irfft(jnp.fft.rfft(uf32, n=2 * seq, axis=1) * k_f[None], n=2 * seq, axis=1)[:, :seq]
    return (y + uf32 * skip.astype(jnp.float32)).astype(u.dtype)

def _hyena(p, k_f, skip):
    parts = jnp.split(p, N_PROJ_B, axis=-1)
    z = parts[0]
    for n in range(HYENA_ORDER):
        z = parts[n + 1] * _long_conv(z, k_f[:, n], skip[n])
    return z

def _token_mix(h, w_in, ln_g, ln_b, w_s, b_s, conv_w, conv_b, fw1, fb1, fw2, fb2, fw3, fb3,
               ffreq, fwo, skip, w_out):
    p = h @ w_in
    u_a, v_a = jnp.split(jax.nn.gelu(p[..., :2 * D_A], approximate=False), 2, axis=-1)
    y_a = _spatial_gating(u_a, v_a, ln_g, ln_b, w_s, b_s)
    p_b = _short_conv(p[..., 2 * D_A:], conv_w, conv_b)
    k_f = _hyena_filter_spectrum(h.shape[1], fw1, fb1, fw2, fb2, fw3, fb3, ffreq, fwo)
    y_b = _hyena(p_b, k_f, skip)
    return jnp.concatenate([y_a, y_b], axis=-1) @ w_out

def setup_inputs(seed: int = 0) -> dict:
    key = jax.random.key(seed)
    ks = iter(jax.random.split(key, 40))

    def nrm(shape, scale):
        return jax.random.normal(next(ks), shape, jnp.float32) * scale

    def gain(shape):
        return 1.0 + nrm(shape, 0.05)

    L = DEPTH
    return {
        'x': nrm((BATCH, SEQ, D_MODEL), 1.0),
        'ffn1_pre_g': gain((L, D_MODEL)),
        'ffn1_w_gate': nrm((L, D_MODEL, D_FF), D_MODEL ** -0.5),
        'ffn1_w_up': nrm((L, D_MODEL, D_FF), D_MODEL ** -0.5),
        'ffn1_w_down': nrm((L, D_FF, D_MODEL), D_FF ** -0.5),
        'ffn1_post_g': gain((L, D_MODEL)),
        'mix_pre_g': gain((L, D_MODEL)),
        'mix_w_in': nrm((L, D_MODEL, IN_COLS), D_MODEL ** -0.5),
        'gmlp_ln_g': gain((L, D_A)),
        'gmlp_ln_b': nrm((L, D_A), 0.02),
        'gmlp_w_s': nrm((L, N_HEADS_A, CHUNK, CHUNK), CHUNK ** -0.5),
        'gmlp_b_s': gain((L, N_HEADS_A, CHUNK)),
        'hy_conv_w': nrm((L, SHORT_K, N_PROJ_B * D_B), SHORT_K ** -0.5),
        'hy_conv_b': nrm((L, N_PROJ_B * D_B), 0.02),
        'hy_filt_w1': nrm((L, FILTER_EMB, FILTER_WIDTH), FILTER_EMB ** -0.5),
        'hy_filt_b1': nrm((L, FILTER_WIDTH), 0.1),
        'hy_filt_w2': nrm((L, FILTER_WIDTH, FILTER_WIDTH), FILTER_WIDTH ** -0.5),
        'hy_filt_b2': nrm((L, FILTER_WIDTH), 0.1),
        'hy_filt_w3': nrm((L, FILTER_WIDTH, FILTER_WIDTH), FILTER_WIDTH ** -0.5),
        'hy_filt_b3': nrm((L, FILTER_WIDTH), 0.1),
        'hy_filt_freq': gain((L, FILTER_WIDTH)),
        'hy_filt_w_out': nrm((L, FILTER_WIDTH, HYENA_ORDER * 2 * D_B), FILTER_OUT_SCALE * FILTER_WIDTH ** -0.5),
        'hy_skip': nrm((L, HYENA_ORDER, D_B), 0.5),
        'mix_w_out': nrm((L, D_MIX, D_MODEL), D_MIX ** -0.5),
        'mix_post_g': gain((L, D_MODEL)),
        'ffn2_pre_g': gain((L, D_MODEL)),
        'ffn2_w_gate': nrm((L, D_MODEL, D_FF), D_MODEL ** -0.5),
        'ffn2_w_up': nrm((L, D_MODEL, D_FF), D_MODEL ** -0.5),
        'ffn2_w_down': nrm((L, D_FF, D_MODEL), D_FF ** -0.5),
        'ffn2_post_g': gain((L, D_MODEL)),
    }

def reference(x, ffn1_pre_g, ffn1_w_gate, ffn1_w_up, ffn1_w_down, ffn1_post_g,
              mix_pre_g, mix_w_in, gmlp_ln_g, gmlp_ln_b, gmlp_w_s, gmlp_b_s,
              hy_conv_w, hy_conv_b, hy_filt_w1, hy_filt_b1, hy_filt_w2, hy_filt_b2,
              hy_filt_w3, hy_filt_b3, hy_filt_freq, hy_filt_w_out, hy_skip,
              mix_w_out, mix_post_g,
              ffn2_pre_g, ffn2_w_gate, ffn2_w_up, ffn2_w_down, ffn2_post_g):
    for l in range(DEPTH):
        h = _rms_norm(x, ffn1_pre_g[l])
        x = x + HALF_STEP * _rms_norm(_swiglu(h, ffn1_w_gate[l], ffn1_w_up[l], ffn1_w_down[l]), ffn1_post_g[l])
        h = _rms_norm(x, mix_pre_g[l])
        y = _token_mix(h, mix_w_in[l], gmlp_ln_g[l], gmlp_ln_b[l], gmlp_w_s[l], gmlp_b_s[l],
                       hy_conv_w[l], hy_conv_b[l], hy_filt_w1[l], hy_filt_b1[l],
                       hy_filt_w2[l], hy_filt_b2[l], hy_filt_w3[l], hy_filt_b3[l],
                       hy_filt_freq[l], hy_filt_w_out[l], hy_skip[l], mix_w_out[l])
        x = x + _rms_norm(y, mix_post_g[l])
        h = _rms_norm(x, ffn2_pre_g[l])
        x = x + HALF_STEP * _rms_norm(_swiglu(h, ffn2_w_gate[l], ffn2_w_up[l], ffn2_w_down[l]), ffn2_post_g[l])
    return x


_drawn_inputs = setup_inputs


def setup_inputs(seed=0):
    import zlib

    import numpy as np

    out = dict(_drawn_inputs(seed))
    spreads = {}
    factors = {'gmlp_ln_b': 4.33}
    for name, (base, spread) in spreads.items():
        noise = np.random.default_rng([zlib.crc32(name.encode()), seed]).standard_normal(out[name].shape)
        drawn = base * np.exp(spread * noise) if base else spread * noise
        out[name] = __import__('jax').numpy.asarray(drawn.astype(out[name].dtype))
    for name, factor in factors.items():
        out[name] = (out[name] * factor).astype(out[name].dtype)
    return out
```

```python
from contextlib import ExitStack

import numpy as np
import concourse.bass as bass
from concourse import mybir

F32 = mybir.dt.float32
F32R = mybir.dt.float32r
I32 = mybir.dt.int32
ALU = mybir.AluOpType
ACT = mybir.ActivationFunctionType

P = 128
SEQ = 512
D_MODEL = 1024
D_FF = 2816
D_B = 512
HEADS = 8
HEAD_DIM = 64
DEPTH = 2
FILTER_EMB = 33
RMS_EPS = 1e-6
LN_EPS = 1e-5

KT = D_MODEL // P
FT = D_FF // P
NT = SEQ // P
HALF_SEQ = SEQ // 2

BLOCK = 1024
UP_BLOCKS = 2 * FT
DOWN_BLOCKS = FT // 2
FFN_BLOCKS = UP_BLOCKS + 2 * DOWN_BLOCKS
MIX_BLOCKS = 40
LAYER_BLOCKS = 2 * FFN_BLOCKS + MIX_BLOCKS
FFN_AT = (0, FFN_BLOCKS + MIX_BLOCKS)
MIX_AT = FFN_BLOCKS
RING = 4
AHEAD = 3
PADDING = RING
assert LAYER_BLOCKS % RING == 0 and UP_BLOCKS % RING == 0 and DOWN_BLOCKS == 11

PRE = (0, 16, 32)
CONV_W = 48
CONV_B = 84
FILT_B = 96
NEXT_PRE = 100
PARAMS = 108

PK_WS = 0
PK_LNG = 1024
PK_LNB = 1536
PK_BS = 2048
PK_W = 2560
PK_Z = 2944
PK_SKIP = 3456
PACK = 3968

ROUND = 1.5 * 2.0 ** 23
PI_BELOW = 3.1415925
TWO_PI = 6.283185307179586

MIX_STEPS = (
    [("z", c, (c,), 1) for c in range(4)]
    + [("v", 0, (4, 5, 6, 7), 4)]
    + [("filter_sum", 0, (), 4)]
    + [("u", c, (8 + c,), 1) for c in (0, 1)]
    + [("filter_diff", 0, (), 4)]
    + [("u", c, (8 + c,), 1) for c in (2, 3)]
    + [("gmlp", 0, (), 4), ("fold", 0, (), 4), ("kernel_cos", 0, (12,), 4), ("kernel_sin", 0, (13,), 4)]
    + [("g1", c, (14 + c,), 1) for c in range(4)]
    + [("forward_low", 0, (18,), 4), ("forward_high", 0, (19,), 4)]
    + [("g2", c, (20 + c,), 1) for c in range(4)]
    + [("inverse", 0, (24, 25), 4), ("filter_sum", 1, (), 4), ("filter_diff", 1, (), 4), ("fold", 1, (), 4)]
    + [("kernel_cos", 1, (26,), 4), ("kernel_sin", 1, (27,), 4)]
    + [("forward_low", 1, (28,), 4), ("forward_high", 1, (29,), 4)]
    + [("cat_a", 0, (), 0), ("out_a", 0, (30, 31), 0), ("inverse", 1, (32, 33), 4)]
)
BANK_SET = {"z": 0, "v": 4, "filter_sum0": 0, "u": 4, "filter_diff0": 0, "fold0": 0, "gmlp": 4,
            "kernel_cos0": 0, "kernel_sin0": 4, "g1": 0, "forward_low0": 4, "forward_high0": 0,
            "g2": 4, "inverse0": 0, "filter_sum1": 4, "filter_diff1": 4, "fold1": 0,
            "kernel_cos1": 4, "kernel_sin1": 0, "forward_low1": 4, "forward_high1": 0, "out_a": 4,
            "inverse1": 0}
RESULTS = sum(s[3] for s in MIX_STEPS)
SIGNALLED = {"v": 3, "filter_sum": 4, "filter_diff": 4, "gmlp": 4, "inverse": 3}
STAGED = {"z": 1, "g1": 1, "g2": 1, "u": 1, "v": 4, "filter_sum": 4, "filter_diff": 4, "fold": 4,
          "kernel_cos": 2, "kernel_sin": 2, "forward_low": 4, "forward_high": 4, "inverse": 4}
VECTOR_LINKS = 170


def bank_set(kind, n):
    return BANK_SET[kind if kind in BANK_SET else f"{kind}{n}"]


def build_encoder(nc, blocks, xt, params, pack, filt_out, skip1, decay, squares, out):
    base = (nc.sbuf_base + 31) // 32 * 32
    place = [base]

    def sb(name, shape, dt=F32, at=None):
        size = 4 * int(np.prod(shape[1:]))
        if at is None:
            at = place[0]
            place[0] += (size + 31) // 32 * 32
        return nc.alloc_sbuf_tensor_at(name, shape, dt, offset=at)

    x = sb("x_t", [P, KT, SEQ])
    h_hi = sb("h_hi", [P, KT, SEQ], F32R)
    h_lo = sb("h_lo", [P, KT, SEQ], F32R)
    y_at = place[0]
    y = sb("y_first_half", [P, 4, SEQ])
    decay_sb = sb("decay_table", [P, 4, SEQ], at=y_at)
    raw = sb("raw_blocks", [P, RING, BLOCK])
    w_hi = sb("block_hi", [P, RING, BLOCK], F32R)
    w_lo = sb("block_lo", [P, RING, BLOCK], F32R)
    act_at = place[0]
    a_hi = sb("hidden_hi", [P, FT, SEQ], F32R)
    a_lo = sb("hidden_lo", [P, FT, SEQ], F32R)
    assert place[0] - act_at == 44 * 2048
    tile = lambda n: act_at + 2048 * n
    zg2 = sb("z_then_gate2", [P, 4, SEQ], at=tile(0))
    g1 = sb("gate1_then_z1", [P, 4, SEQ], at=tile(4))
    u = sb("gmlp_u", [P, 4, SEQ], at=tile(8))
    v = sb("gmlp_v", [P, NT, SEQ], at=tile(12))
    fold_lo = sb("fold_lo", [P, 4, SEQ], F32R, at=tile(12))
    k_spec = sb("kernel_spectrum", [P, 8, SEQ], at=tile(16))
    pk = sb("mixer_pack", [P, PACK], at=tile(16))
    s_hi = sb("filter_or_spectrum_hi", [P, 8, SEQ], F32R, at=tile(24))
    s_lo = sb("filter_or_spectrum_lo", [P, 8, SEQ], F32R, at=tile(32))
    fold_hi = sb("fold_hi", [P, 4, SEQ], F32R, at=tile(40))
    scale_b = sb("rms_scale", [P, SEQ])
    T = [sb(f"work{i}", [P, SEQ]) for i in range(4)]
    hid = sb("square_sum_or_filter_hidden", [P, SEQ])
    wo = sb("filter_out_weights", [P, D_B])
    ident = sb("identity", [P, P])
    ones = sb("ones", [P, P])
    par = sb("layer_params", [P, PARAMS])
    mean_sq = sb("mean_square", [P, NT])
    newton = sb("newton_term", [P, NT])
    rcol = sb("rms_scale_columns", [P, NT])
    stats = sb("ln_stats", [P, NT, 6])
    mv = sb("ln_mean_var", [P, NT, 2])
    rstd = sb("ln_rstd", [P, NT])
    assert place[0] <= nc.sbuf_usable_end, (place[0], nc.sbuf_usable_end)

    with ExitStack() as ctx:
        bank = [ctx.enter_context(nc.psum_tensor(f"bank{i}", [P, SEQ], F32)) for i in range(8)]

        def sem(name):
            return ctx.enter_context(nc.semaphore(name))

        landed = [sem(f"block_landed{i}") for i in range(RING)]
        x_loaded = [sem(f"x_loaded{i}") for i in range(4)]
        tables_loaded = sem("tables_loaded")
        params_loaded = sem("params_loaded")
        pack_loaded = sem("pack_loaded")
        filt_loaded = sem("filter_out_loaded")
        skip_loaded = sem("skip_loaded")
        decay_loaded = sem("decay_loaded")
        stored = sem("out_stored")
        block_hi = sem("block_hi_ready")
        block_split = sem("block_split")
        block_used = sem("block_used")
        x_ready = sem("x_updated")
        h_hi_ready = sem("h_hi_ready")
        h_ready = sem("h_split")
        square_ready = sem("square_ready")
        summed = sem("squares_summed")
        cols_ready = sem("mean_square_columns")
        diag_ready = sem("scale_diagonal")
        scale_ready = sem("scale_broadcast")
        scale_twin = sem("scale_broadcast_twin")
        scale_copied = sem("scale_in_sbuf")
        bank_scaled = sem("gate_up_scaled")
        silu_ready = sem("silu_ready")
        hidden_ready = sem("hidden_ready")
        hidden_hi = sem("hidden_hi_ready")
        hidden_split = sem("hidden_split")
        y_done = sem("y_bank_done")
        chain = sem("vector_step")
        ln_chain = sem("pool_step")
        load_go = sem("small_load_may_start")
        stats_go = sem("ln_stats_seen")
        result = sem("mixer_result")
        result_read = sem("mixer_result_read")
        staged = sem("mixer_result_staged")
        mlp_done = sem("filter_mlp_done")
        mlp_arg = sem("filter_mlp_argument")
        mlp_sin = sem("filter_mlp_sine")
        hid_ready = sem("filter_hidden_ready")
        negated = sem("filter_out_negated")
        filter_split = sem("filter_split")
        fold_ready = sem("fold_ready")
        fold_turned = sem("fold_transposed")
        spectrum_split = sem("spectrum_split")
        ln_centred = sem("ln_centred")
        ln_ready = sem("ln_ready")
        gmlp_ready = sem("gmlp_ready")
        gated = sem("hyena_gated")
        cat_hi = sem("cat_hi_ready")
        cat_split = sem("cat_split")
        block = ctx.enter_context(nc.Block())

        def n_block(l, k):
            return l * LAYER_BLOCKS + k

        def n_landed(l, k):
            return (l * (LAYER_BLOCKS // RING) + (k // RING) + 1) * 16

        def n_tile(l, s, k):
            return l * 24 + (8 * s + k)

        def n_updated(l, s, k):
            return l * 24 + (8 * s + k + 1)

        def n_columns(l, s, post):
            return l * 6 + (2 * s + post + 1)

        def n_summed(l, s, post, k):
            return l * 36 + (6 * (2 * s + post) + k + 1)

        def n_square(l, s, post, k):
            return l * 48 + (16 * s + 8 * post + k)

        def n_norm(l, s, post):
            return l * 6 + (2 * s + post)

        def n_hidden(l, part, f):
            return l * (2 * FT) + (FT * part + f)

        def bases(count):
            at = [0]
            for step in MIX_STEPS:
                at.append(at[-1] + count(step))
            return at

        base_of = bases(lambda step: step[3])
        signalled_of = bases(lambda step: SIGNALLED.get(step[0], 0))
        staged_of = bases(lambda step: STAGED.get(step[0], 0))

        def n_read(l, e, i):
            return l * RESULTS + (base_of[e] + i)

        def n_staged(l, e, i):
            return l * staged_of[-1] + (staged_of[e] + i)

        def wait_block(eng, l, k):
            eng.wait_ge(block_used, n_block(l, k + 1) + RING)

        def wait_result(eng, l, e, i):
            kind, n, blks, m = MIX_STEPS[e]
            if kind == "fold":
                eng.wait_ge(fold_turned, l * 8 + 4 * (n + 1))
            elif blks and (i == m or kind not in SIGNALLED):
                wait_block(eng, l, MIX_AT + blks[-1])
            else:
                eng.wait_ge(result, l * signalled_of[-1] + (signalled_of[e] + i))

        def n_y_done(l, s, half, d):
            return l * 18 + (6 * s + 3 * half + d)

        def last_down(s, half):
            if s == 1:
                return MIX_AT + 35 + 4 * half
            return FFN_AT[s // 2] + UP_BLOCKS + (half + 1) * DOWN_BLOCKS - 1

        def last_in_bank(e, b):
            for d in range(e - 1, -1, -1):
                kind, n, _, m = MIX_STEPS[d]
                first = bank_set(kind, n) if m else 99
                if m == 1 and first + n == b:
                    return base_of[d]
                if m == 4 and first <= b < first + 4:
                    return base_of[d] + 3
            return None

        @block.sync
        def _(sp):
            with sp.Fori(0, (DEPTH * LAYER_BLOCKS + PADDING) // RING) as r:
                for j in range(RING):
                    sp.wait_ge(block_split, r * RING + (j + 1))
                    sp.dma_start(raw[:, j], blocks[r * RING + j]).then_inc(landed[j], 16)
            for k in range(KT):
                sp.wait_ge(x_ready, n_updated(DEPTH - 1, 2, k + 1))
                sp.dma_start(out[:, k], x[:, k]).then_inc(stored, 16)
            sp.wait_ge(stored, 16 * KT)

        @block.gpsimd
        def _(pool):
            pool.sem_inc(summed, 1)
            pool.dma_start(par[:], params[0]).then_inc(params_loaded, 16)
            pool.dma_start(ident[:], squares[0]).then_inc(tables_loaded, 16)
            pool.dma_start(ones[:], squares[1]).then_inc(tables_loaded, 16)

            def sum_squares(l, s, post):
                pool.wait_ge(cols_ready, n_columns(l, s, post))
                for k in range(1, KT - 1):
                    pool.wait_ge(square_ready, n_square(l, s, post, k + 1))
                    first = T[2][:] if k == 1 else hid[:]
                    if k > 1:
                        pool.wait_ge(summed, n_summed(l, s, post, k - 1))
                    nc.gpsimd.tensor_tensor(hid[:], first, T[2 + k % 2][:], ALU.add).then_inc(summed, 1)

            for k in range(1, KT - 1):
                pool.wait_ge(square_ready, k + 1)
                if k > 1:
                    pool.wait_ge(summed, k)
                nc.gpsimd.tensor_tensor(hid[:], T[2][:] if k == 1 else hid[:], T[2 + k % 2][:], ALU.add)\
                    .then_inc(summed, 1)
            with pool.Fori(0, DEPTH) as l:
                pool.wait_ge(h_ready, n_tile(l, 0, 8))
                pool.sem_inc(load_go, 1)
                pool.dma_start(par[:], params[l]).then_inc(params_loaded, 16)
                sum_squares(l, 0, 1)
                wait_block(pool, l, last_down(0, 1))
                pool.sem_inc(load_go, 1)
                pool.dma_start(pk[:], pack[l]).then_inc(pack_loaded, 16)
                pool.dma_start(wo[:], filt_out[l * 2]).then_inc(filt_loaded, 16)
                sum_squares(l, 1, 0)
                pool.wait_ge(x_ready, n_updated(l, 0, 8))
                pool.sem_inc(load_go, 1)
                pool.dma_start(decay_sb[:], decay).then_inc(decay_loaded, 16)
                pool.wait_ge(pack_loaded, (l + 1) * 16)
                for t in range(NT):
                    pool.wait_ge(ln_centred, l * NT + (t + 1))
                    nc.gpsimd.tensor_tensor(v[:, t], v[:, t], pk[:, PK_LNG:PK_LNG + 512], ALU.mult)\
                        .then_inc(ln_chain, 1)
                    pool.wait_ge(ln_chain, l * NT + (t + 1))
                    nc.gpsimd.tensor_tensor(v[:, t], v[:, t], pk[:, PK_LNB:PK_LNB + 512], ALU.add)\
                        .then_inc(ln_ready, 1)
                e = MIX_STEPS.index(("filter_diff", 0, (), 4))
                wait_result(pool, l, e, 4)
                pool.sem_inc(load_go, 1)
                pool.dma_start(wo[:], filt_out[l * 2 + 1]).then_inc(filt_loaded, 16)
                e = MIX_STEPS.index(("g2", 3, (23,), 1))
                pool.wait_ge(result_read, n_read(l, e, 1))
                pool.sem_inc(load_go, 1)
                pool.dma_start(scale_b[0:1, :], skip1[l]).then_inc(skip_loaded, 16)
                sum_squares(l, 1, 1)
                sum_squares(l, 2, 0)
                sum_squares(l, 2, 1)
                sum_squares(l + 1, 0, 0)

        @block.scalar
        def _(act):
            def split_hi(l, k, slot=None):
                slot = k % RING if slot is None else slot
                act.wait_ge(landed[slot], n_landed(l, k))
                act.wait_ge(block_used, n_block(l, k + 1))
                nc.scalar.activation(w_hi[:, slot], raw[:, slot], ACT.Copy).then_inc(block_hi, 1)

            def square_tile(l, s, post, k, src):
                if k < 2:
                    act.wait_ge(cols_ready, n_columns(l, s, post))
                else:
                    act.wait_ge(summed, n_summed(l, s, post, max(k - 2, 1)))
                nc.scalar.activation(T[2 + k % 2][:], src, ACT.Square).then_inc(square_ready, 1)

            def before(l, s, gain):
                after = (l, s + 1) if s < 2 else (l + 1, 0)
                act.wait_ge(scale_twin, l * 3 + (s + 1))
                nc.scalar.activation(scale_b[:], bank[1][:], ACT.Copy).then_inc(scale_copied, 1)
                for k in range(KT):
                    act.wait_ge(x_ready, n_updated(l, s, k + 1))
                    nc.scalar.activation(h_hi[:, k], x[:, k], ACT.Copy,
                                         scale=par[:, gain + k:gain + k + 1]).then_inc(h_hi_ready, 1)
                    square_tile(*after, 0, k, x[:, k])

            def after_half(l, s, half):
                for d in range(4):
                    k = 4 * half + d
                    if d < 3:
                        act.wait_ge(y_done, n_y_done(l, s, half, d + 1))
                    else:
                        wait_block(act, l, last_down(s, half))
                    if half == 0:
                        nc.scalar.activation(y[:, d], bank[4 + d][:], ACT.Copy)
                    square_tile(l, s, 1, k, bank[4 + d][:])

            def hidden(l, part, f):
                act.wait_ge(bank_scaled, n_hidden(l, part, f) * 2 + 1)
                nc.scalar.activation(T[1][:], T[0][:], ACT.Silu).then_inc(silu_ready, 1)
                act.wait_ge(hidden_ready, n_hidden(l, part, f) + 1)
                nc.scalar.activation(a_hi[:, f], T[3][:], ACT.Copy).then_inc(hidden_hi, 1)

            def ffn(l, part):
                k0 = FFN_AT[part]
                s = 2 * part
                for f in (0, 1):
                    split_hi(l, k0 + 2 * f + AHEAD)
                    split_hi(l, k0 + 2 * f + 1 + AHEAD)
                    hidden(l, part, f)
                with act.Fori(0, UP_BLOCKS // RING - 1) as i:
                    for f in (2, 3):
                        for b in (0, 1):
                            j = k0 + 2 * f + b + AHEAD
                            act.wait_ge(landed[j % RING],
                                        (l * (LAYER_BLOCKS // RING) + i + (j // RING + 1)) * 16)
                            act.wait_ge(block_used, l * LAYER_BLOCKS + i * RING + (j + 1))
                            nc.scalar.activation(w_hi[:, j % RING], raw[:, j % RING], ACT.Copy)\
                                .then_inc(block_hi, 1)
                        n = l * (2 * FT) + i * 2 + (FT * part + f)
                        act.wait_ge(bank_scaled, n * 2 + 1)
                        nc.scalar.activation(T[1][:], T[0][:], ACT.Silu).then_inc(silu_ready, 1)
                        act.wait_ge(hidden_ready, n + 1)
                        nc.scalar.activation(a_hi[:, i * 2 + f], T[3][:], ACT.Copy).then_inc(hidden_hi, 1)
                for half in (0, 1):
                    down(l, s, k0 + UP_BLOCKS + half * DOWN_BLOCKS, half)

            def down(l, s, k1, half):
                split_hi(l, k1 + AHEAD)
                with act.Fori(0, 2) as i:
                    for b in range(RING):
                        j = k1 + 1 + b + AHEAD
                        act.wait_ge(landed[j % RING],
                                    (l * (LAYER_BLOCKS // RING) + i + (j // RING + 1)) * 16)
                        act.wait_ge(block_used, l * LAYER_BLOCKS + i * RING + (j + 1))
                        nc.scalar.activation(w_hi[:, j % RING], raw[:, j % RING], ACT.Copy)\
                            .then_inc(block_hi, 1)
                for b in (9, 10):
                    split_hi(l, k1 + b + AHEAD)
                after_half(l, s, half)

            def mix_step(l, e):
                kind, n, blks, _ = MIX_STEPS[e]
                for k in blks:
                    split_hi(l, MIX_AT + k + AHEAD)
                    if kind == "v" and k < 7:
                        m = k - 4
                        act.wait_ge(mlp_arg, l * 3 + (m + 1))
                        nc.scalar.activation(hid[:] if m == 2 else T[2][:], T[0][:], ACT.Sin)\
                            .then_inc(mlp_sin, 1)
                first = bank_set(kind, n) if kind != "cat_a" else 0
                if kind == "z" and n < 2:
                    pass
                elif kind == "z" and n == 2:
                    for m in (0, 1, 2):
                        middle_tap(l, e - 2 + m, kind, m)
                elif kind in ("z", "g1", "g2"):
                    middle_tap(l, e, kind, n)
                elif kind == "v":
                    for t in range(NT):
                        wait_result(act, l, e, t + 1)
                        nc.scalar.activation(v[:, t], bank[first + t][:], ACT.Gelu,
                                             scale=rcol[:, t:t + 1]).then_inc(staged, 1)
                elif kind == "u":
                    act.wait_ge(result_read, n_read(l, e, 1))
                    nc.scalar.activation(u[:, n], T[n % 2][:], ACT.Gelu).then_inc(staged, 1)
                elif kind in ("filter_sum", "filter_diff"):
                    for j in range(4):
                        act.wait_ge(result_read, n_read(l, e, j + 1))
                        q = j + 4 * (kind == "filter_diff")
                        nc.scalar.activation(s_hi[:, q], T[j % 2][:], ACT.Copy).then_inc(staged, 1)
                elif kind == "fold":
                    for q in range(4):
                        wait_result(act, l, e, 4)
                        nc.scalar.activation(fold_hi[:, q], bank[first + q][:], ACT.Copy).then_inc(staged, 1)
                elif kind in ("kernel_cos", "kernel_sin"):
                    wait_result(act, l, e, 4)
                    if kind == "kernel_sin":
                        act.wait_ge(result_read, n_read(l, e, 0))
                    elif n == 0:
                        act.wait_ge(gmlp_ready, l * 4 + 4)
                    for i in (0, 1):
                        nc.scalar.activation(T[i][:], bank[first + i][:], ACT.Copy).then_inc(staged, 1)
                elif kind in ("forward_low", "forward_high"):
                    for i in (0, 1):
                        q = i + 2 * (kind == "forward_high")
                        for part in (0, 1):
                            act.wait_ge(result_read, n_read(l, e, 2 * i + part + 1))
                            nc.scalar.activation(s_hi[:, 4 * part + q], T[2 * part][:], ACT.Copy)\
                                .then_inc(staged, 1)
                elif kind == "inverse":
                    for c in range(4):
                        wait_result(act, l, e, c + 1)
                        if c >= 2:
                            act.wait_ge(result_read, n_read(l, e, c - 1))
                        nc.scalar.activation(T[2 + c % 2][:, 0:HALF_SEQ], bank[first + c][:, 0:HALF_SEQ],
                                             ACT.Copy).then_inc(staged, 1)
                        if n == 1 and c >= 1:
                            cat_yb(l, c - 1)
                    if n == 1:
                        cat_yb(l, 3)
                elif kind == "cat_a":
                    for c in range(4):
                        act.wait_ge(gmlp_ready, l * 4 + (c + 1))
                        nc.scalar.activation(h_hi[:, c], u[:, c], ACT.Copy).then_inc(cat_hi, 1)

            def middle_tap(l, e, kind, n):
                c = n + {"z": 0, "g1": 4, "g2": 8}[kind]
                dst = {"z": zg2, "g1": g1, "g2": zg2}[kind]
                act.wait_ge(result_read, n_read(l, e, 1))
                nc.scalar.activation(dst[:, n], T[n % 2][:], ACT.Identity,
                                     bias=par[:, CONV_B + c:CONV_B + c + 1],
                                     scale=par[:, CONV_W + 12 + c:CONV_W + 13 + c]).then_inc(staged, 1)

            def cat_yb(l, c):
                act.wait_ge(gated, l * 4 + (c + 1))
                nc.scalar.activation(h_hi[:, 4 + c], T[c % 2][:], ACT.Copy).then_inc(cat_hi, 1)

            for i in range(4):
                act.dma_start(x[:, 2 * i:2 * i + 2], xt[:, 2 * i:2 * i + 2]).then_inc(x_loaded[i], 16)
            act.wait_ge(params_loaded, 16)
            for k in range(KT):
                if k in (0, 1, 2):
                    act.wait_ge(landed[k], 16)
                    nc.scalar.activation(w_hi[:, k], raw[:, k], ACT.Copy).then_inc(block_hi, 1)
                if k % 2 == 0:
                    act.wait_ge(x_loaded[k // 2], 16)
                nc.scalar.activation(h_hi[:, k], x[:, k], ACT.Copy, scale=par[:, k:k + 1]).then_inc(h_hi_ready, 1)
                if k >= 2:
                    act.wait_ge(summed, max(k - 2, 1) + 1)
                nc.scalar.activation(T[2 + k % 2][:], x[:, k], ACT.Square).then_inc(square_ready, 1)
            with act.Fori(0, DEPTH) as l:
                ffn(l, 0)
                act.wait_ge(params_loaded, (l + 2) * 16)
                before(l, 0, PRE[1])
                for e in range(len(MIX_STEPS)):
                    mix_step(l, e)
                for k in range(34, 40):
                    split_hi(l, MIX_AT + k + AHEAD)
                    if k == 35:
                        after_half(l, 1, 0)
                after_half(l, 1, 1)
                before(l, 1, PRE[2])
                ffn(l, 1)
                before(l, 2, NEXT_PRE)

        @block.vector
        def _(vec):
            links = [0]

            def link(l, ins):
                links[0] += 1
                ins.then_inc(chain, 1)
                vec.wait_ge(chain, l * VECTOR_LINKS + links[0])

            def split_lo(l, k, slot=None):
                slot = k % RING
                vec.wait_ge(block_hi, n_block(l, k + 1))
                nc.vector.tensor_tensor(w_lo[:, slot], raw[:, slot], w_hi[:, slot], ALU.subtract)\
                    .then_inc(block_split, 1)

            def h_low(n, k, gain):
                vec.wait_ge(h_hi_ready, n)
                nc.vector.scalar_tensor_tensor(h_lo[:, k], x[:, k], par[:, gain + k:gain + k + 1],
                                               h_hi[:, k], ALU.mult, ALU.subtract).then_inc(h_ready, 1)

            def inverse_root(l, dst):
                guess = dst.bitcast(I32)
                link(l, nc.vector.tensor_scalar(guess, mean_sq[:].bitcast(I32), 1, None,
                                                ALU.logical_shift_right))
                link(l, nc.vector.tensor_scalar(guess, guess, -1, 0x5F3759DF, ALU.mult, ALU.add))
                for _ in range(3):
                    link(l, nc.vector.tensor_tensor(newton[:], dst, dst, ALU.mult))
                    link(l, nc.vector.scalar_tensor_tensor(newton[:], newton[:], -0.5, mean_sq[:],
                                                           ALU.mult, ALU.mult))
                    link(l, nc.vector.scalar_tensor_tensor(dst, newton[:], 1.5, dst, ALU.add, ALU.mult))

            def scale_columns(l, s, post):
                src = bank[2 if post else 4]
                vec.wait_ge(cols_ready, n_columns(l, s, post) + 1)
                link(l, nc.vector.tensor_scalar(mean_sq[:], src[:, 0:NT], 1.0 / D_MODEL, RMS_EPS,
                                                ALU.mult, ALU.add))
                inverse_root(l, rcol[:])
                nc.vector.tensor_tensor(
                    T[0][:].rearrange("p (t j) -> p t j", t=NT),
                    ident[:].unsqueeze(1).broadcast_to([P, NT, P]),
                    rcol[:].unsqueeze(2).broadcast_to([P, NT, P]), ALU.mult).then_inc(diag_ready, 1)

            def scale_tile(l, s, post):
                vec.wait_ge(scale_ready, n_norm(l, s, post) + 1)
                link(l, nc.vector.tensor_copy(scale_b[:], bank[3 if post else 5][:]))

            def update(l, s):
                scale_columns(l, s, 1)
                vec.wait_ge(scale_ready, n_norm(l, s, 1) + 1)
                gain = (PRE[1], PRE[2], NEXT_PRE)[s]
                for k in range(KT):
                    if k == 1:
                        vec.wait_ge(scale_twin, l * 3 + (s + 1))
                    if k == 4:
                        vec.wait_ge(scale_copied, l * 3 + (s + 1))
                    src, scale = (y[:, k], bank[3][:]) if k < 4 else (bank[k][:], scale_b[:])
                    g = PRE[s] + 8 + k
                    link(l, nc.vector.scalar_tensor_tensor(T[(k + 1) % 2][:], src, par[:, g:g + 1], scale,
                                                           ALU.mult, ALU.mult))
                    nc.vector.tensor_tensor(x[:, k], x[:, k], T[(k + 1) % 2][:], ALU.add).then_inc(x_ready, 1)
                    if k:
                        h_low(n_tile(l, s + 1, k), k - 1, gain)
                h_low(n_tile(l, s + 1, KT), KT - 1, gain)

            def gate(l, part, n, f, used_at):
                vec.wait_ge(block_used, used_at)
                nc.vector.tensor_tensor(T[0][:], bank[2 * (f % 2)][:], scale_b[:], ALU.mult)\
                    .then_inc(bank_scaled, 1)

            def hidden(l, part, n, f, f_at, used_at):
                vec.wait_ge(block_used, used_at)
                nc.vector.tensor_tensor(T[2][:], bank[2 * (f % 2) + 1][:], scale_b[:], ALU.mult)\
                    .then_inc(bank_scaled, 1)
                vec.wait_ge(silu_ready, n + 1)
                vec.wait_ge(bank_scaled, n * 2 + 2)
                nc.vector.tensor_tensor(T[3][:], T[1][:], T[2][:], ALU.mult).then_inc(hidden_ready, 1)
                vec.wait_ge(hidden_hi, n + 1)
                nc.vector.tensor_tensor(a_lo[:, f_at], T[3][:], a_hi[:, f_at], ALU.subtract)\
                    .then_inc(hidden_split, 1)

            def ffn(l, part):
                k0 = FFN_AT[part]
                s = 2 * part
                split_lo(l, k0 + 3)
                scale_columns(l, s, 0)
                split_lo(l, k0 + 4)
                scale_tile(l, s, 0)
                at = lambda b: n_block(l, k0 + b + 1) + RING
                gate(l, part, n_hidden(l, part, 0), 0, at(0))
                hidden(l, part, n_hidden(l, part, 0), 0, 0, at(1))
                split_lo(l, k0 + 5)
                gate(l, part, n_hidden(l, part, 1), 1, at(2))
                split_lo(l, k0 + 6)
                hidden(l, part, n_hidden(l, part, 1), 1, 1, at(3))
                with vec.Fori(0, UP_BLOCKS // RING - 1) as i:
                    for f in (2, 3):
                        n = l * (2 * FT) + i * 2 + (FT * part + f)
                        for b in (0, 1):
                            j = k0 + 2 * f + b + AHEAD
                            vec.wait_ge(block_hi, l * LAYER_BLOCKS + i * RING + (j + 1))
                            nc.vector.tensor_tensor(w_lo[:, j % RING], raw[:, j % RING], w_hi[:, j % RING],
                                                    ALU.subtract).then_inc(block_split, 1)
                            done = l * LAYER_BLOCKS + i * RING + (k0 + 2 * f + b + 1 + RING)
                            if b == 0:
                                gate(l, part, n, f, done)
                            else:
                                hidden(l, part, n, f, i * 2 + f, done)
                if part == 0:
                    vec.wait_ge(params_loaded, (l + 2) * 16)
                    for g in (PRE[0] + 8, PRE[2] + 8):
                        link(l, nc.vector.tensor_scalar(par[:, g:g + 8], par[:, g:g + 8], 0.5, None, ALU.mult))
                for half in (0, 1):
                    k1 = k0 + UP_BLOCKS + half * DOWN_BLOCKS
                    split_lo(l, k1 + AHEAD)
                    with vec.Fori(0, 2) as i:
                        for b in range(RING):
                            j = k1 + 1 + b + AHEAD
                            vec.wait_ge(block_hi, l * LAYER_BLOCKS + i * RING + (j + 1))
                            nc.vector.tensor_tensor(w_lo[:, j % RING], raw[:, j % RING], w_hi[:, j % RING],
                                                    ALU.subtract).then_inc(block_split, 1)
                    for b in (9, 10):
                        split_lo(l, k1 + b + AHEAD)
                update(l, s)

            def mlp_argument(l, m):
                vec.wait_ge(mlp_done, l * 3 + (m + 1))
                link(l, nc.vector.tensor_scalar(T[0][:], bank[m][:], par[:, FILT_B + m:FILT_B + m + 1],
                                                par[:, FILT_B + 3:FILT_B + 4], ALU.add, ALU.mult))
                link(l, nc.vector.tensor_scalar(T[1][:], T[0][:], 1.0 / TWO_PI, ROUND, ALU.mult, ALU.add))
                link(l, nc.vector.tensor_scalar(T[1][:], T[1][:], ROUND, -TWO_PI, ALU.subtract, ALU.mult))
                link(l, nc.vector.tensor_tensor(T[0][:], T[0][:], T[1][:], ALU.add))
                nc.vector.tensor_scalar(T[0][:], T[0][:], PI_BELOW, -PI_BELOW, ALU.min, ALU.max)\
                    .then_inc(mlp_arg, 1)
                if m == 2:
                    vec.wait_ge(mlp_sin, l * 3 + 3)
                    nc.vector.memset(hid[HEAD_DIM:P, 0:1], 0.0).then_inc(hid_ready, 1)

            def mix_step(l, e):
                kind, n, blks, _ = MIX_STEPS[e]
                first = bank_set(kind, n) if kind != "cat_a" else 0
                for k in blks:
                    split_lo(l, MIX_AT + k + AHEAD)
                    if kind == "v" and k < 7:
                        mlp_argument(l, k - 4)
                if kind == "z" and n == 1:
                    scale_columns(l, 1, 0)
                    return
                if kind == "z" and n == 2:
                    scale_tile(l, 1, 0)
                    for m in (0, 1, 2):
                        projection(l, e - 2 + m, "z", m, bank[m])
                    return
                if kind == "z" and n == 0:
                    return
                if kind in ("z", "g1", "g2"):
                    projection(l, e, kind, n, bank[first + n])
                elif kind == "v":
                    for t in range(NT):
                        vec.wait_ge(staged, n_staged(l, e, t + 1))
                        nc.vector.bn_stats(stats[:, t], v[:, t]).then_inc(result_read, 1)
                    vec.wait_ge(result_read, n_read(l, e, 4))
                    vec.sem_inc(stats_go, 1)
                    for t in range(NT):
                        ins = nc.vector.bn_aggr(mv[:, t], stats[:, t])
                    link(l, ins)
                    link(l, nc.vector.tensor_scalar(mean_sq[:], mv[:, :, 1], LN_EPS, None, ALU.add))
                    inverse_root(l, rstd[:])
                    for t in range(NT):
                        nc.vector.tensor_scalar(v[:, t], v[:, t], mv[:, t, 0:1], rstd[:, t:t + 1],
                                                ALU.subtract, ALU.mult).then_inc(ln_centred, 1)
                elif kind == "u":
                    wait_result(vec, l, e, 1)
                    nc.vector.tensor_tensor(T[n % 2][:], bank[first + n][:], scale_b[:], ALU.mult)\
                        .then_inc(result_read, 1)
                    vec.wait_ge(staged, n_staged(l, e, 1))
                elif kind in ("filter_sum", "filter_diff"):
                    diff = kind == "filter_diff"
                    vec.wait_ge(decay_loaded, (l + 1) * 16)
                    for j in range(4):
                        wait_result(vec, l, e, j + 1)
                        nc.vector.tensor_tensor(T[j % 2][:], bank[first + j][:], decay_sb[:, j], ALU.mult)\
                            .then_inc(result_read, 1)
                        vec.wait_ge(staged, n_staged(l, e, j + 1))
                        nc.vector.tensor_tensor(s_lo[:, j + 4 * diff], T[j % 2][:], s_hi[:, j + 4 * diff],
                                                ALU.subtract).then_inc(filter_split, 1)
                    vec.wait_ge(filter_split, l * 16 + (8 * n + 4 * diff + 4))
                    if not diff:
                        nc.vector.tensor_scalar(wo[HEAD_DIM:P, :], wo[HEAD_DIM:P, :], -1.0, None, ALU.mult)\
                            .then_inc(negated, 1)
                elif kind == "fold":
                    src = g1 if n else zg2
                    for c in range(4):
                        if c >= 2:
                            vec.wait_ge(fold_turned, l * 8 + (4 * n + c - 1))
                        late, early = src[:, c, HALF_SEQ:SEQ], src[:, c, HALF_SEQ - 1::-1]
                        nc.vector.tensor_tensor(T[2 + c % 2][:, 0:HALF_SEQ], late, early, ALU.add)
                        nc.vector.tensor_tensor(T[2 + c % 2][:, HALF_SEQ:SEQ], late, early, ALU.subtract)\
                            .then_inc(fold_ready, 1)
                    for q in range(4):
                        vec.wait_ge(staged, n_staged(l, e, q + 1))
                        nc.vector.tensor_tensor(fold_lo[:, q], bank[first + q][:], fold_hi[:, q],
                                                ALU.subtract).then_inc(result_read, 1)
                elif kind == "gmlp":
                    for c in range(4):
                        wait_result(vec, l, e, c + 1)
                        bias = pk[:, PK_BS + c * P:PK_BS + (c + 1) * P].unsqueeze(1).broadcast_to([P, NT, P])
                        nc.vector.tensor_tensor(T[c % 2][:].rearrange("p (t j) -> p t j", t=NT),
                                                bank[first + c][:].rearrange("p (t j) -> p t j", t=NT),
                                                bias, ALU.add).then_inc(result_read, 1)
                        vec.wait_ge(result_read, n_read(l, e, c + 1))
                        nc.vector.tensor_tensor(u[:, c], T[c % 2][:], u[:, c], ALU.mult).then_inc(gmlp_ready, 1)
                elif kind in ("kernel_cos", "kernel_sin"):
                    o = 4 * (kind == "kernel_sin")
                    for i in (0, 1):
                        vec.wait_ge(staged, n_staged(l, e, i + 1))
                        odd = bank[first + 2 + i][:]
                        nc.vector.tensor_tensor(k_spec[:, o + i], T[i][:], odd, ALU.add).then_inc(result_read, 1)
                        if o:
                            ins = nc.vector.scalar_tensor_tensor(k_spec[:, o + 2 + i], T[i][:], -1.0, odd,
                                                                 ALU.mult, ALU.add)
                        else:
                            ins = nc.vector.tensor_tensor(k_spec[:, o + 2 + i], T[i][:], odd, ALU.subtract)
                        ins.then_inc(result_read, 1)
                    vec.wait_ge(result_read, n_read(l, e, 4))
                elif kind in ("forward_low", "forward_high"):
                    for i in (0, 1):
                        q = i + 2 * (kind == "forward_high")
                        re, im = bank[first + i][:], bank[first + 2 + i][:]
                        k_re, k_im = k_spec[:, q], k_spec[:, 4 + q]
                        wait_result(vec, l, e, 4)
                        nc.vector.tensor_tensor(T[0][:], re, k_re, ALU.mult)
                        nc.vector.tensor_tensor(T[2][:], re, k_im, ALU.mult)
                        link(l, nc.vector.tensor_tensor(T[1][:], im, k_im, ALU.mult))
                        nc.vector.tensor_tensor(T[0][:], T[0][:], T[1][:], ALU.subtract).then_inc(result_read, 1)
                        link(l, nc.vector.tensor_tensor(T[3][:], im, k_re, ALU.mult))
                        nc.vector.tensor_tensor(T[2][:], T[2][:], T[3][:], ALU.add).then_inc(result_read, 1)
                        for part in (0, 1):
                            vec.wait_ge(staged, n_staged(l, e, 2 * i + part + 1))
                            nc.vector.tensor_tensor(s_lo[:, 4 * part + q], T[2 * part][:],
                                                    s_hi[:, 4 * part + q], ALU.subtract)\
                                .then_inc(spectrum_split, 1)
                        vec.wait_ge(spectrum_split, l * 16 + (8 * n + 2 * q + 2))
                elif kind == "inverse":
                    for c in range(4):
                        vec.wait_ge(staged, n_staged(l, e, c + 1))
                        even, odd = T[2 + c % 2][:, 0:HALF_SEQ], bank[first + c][:, HALF_SEQ:SEQ]
                        nc.vector.tensor_tensor(T[c % 2][:, HALF_SEQ:SEQ], even, odd, ALU.subtract)
                        nc.vector.tensor_tensor(T[c % 2][:, HALF_SEQ - 1::-1], even, odd, ALU.add)\
                            .then_inc(result_read, 1)
                        vec.wait_ge(result_read, n_read(l, e, c + 1))
                        if n == 0:
                            link(l, nc.vector.tensor_tensor(g1[:, c], g1[:, c], T[c % 2][:], ALU.mult))
                        else:
                            nc.vector.tensor_tensor(T[c % 2][:], zg2[:, c], T[c % 2][:], ALU.mult)\
                                .then_inc(gated, 1)
                            vec.wait_ge(cat_hi, l * 8 + (4 + c + 1))
                            nc.vector.tensor_tensor(h_lo[:, 4 + c], T[c % 2][:], h_hi[:, 4 + c],
                                                    ALU.subtract).then_inc(cat_split, 1)
                elif kind == "cat_a":
                    for c in range(4):
                        vec.wait_ge(cat_hi, l * 8 + (c + 1))
                        nc.vector.tensor_tensor(h_lo[:, c], u[:, c], h_hi[:, c], ALU.subtract)\
                            .then_inc(cat_split, 1)

            def projection(l, e, kind, n, src):
                c = n + {"z": 0, "g1": 4, "g2": 8}[kind]
                dst = {"z": zg2, "g1": g1, "g2": zg2}[kind]
                wait_result(vec, l, e, 1)
                nc.vector.tensor_tensor(T[n % 2][:], src[:], scale_b[:], ALU.mult).then_inc(result_read, 1)
                vec.wait_ge(staged, n_staged(l, e, 1))
                link(l, nc.vector.scalar_tensor_tensor(
                    dst[:, n, 1:SEQ], T[n % 2][:, 0:SEQ - 1], par[:, CONV_W + c:CONV_W + c + 1],
                    dst[:, n, 1:SEQ], ALU.mult, ALU.add))
                link(l, nc.vector.scalar_tensor_tensor(
                    dst[:, n, 0:SEQ - 1], T[n % 2][:, 1:SEQ], par[:, CONV_W + 24 + c:CONV_W + 25 + c],
                    dst[:, n, 0:SEQ - 1], ALU.mult, ALU.add))

            nc.vector.sem_inc(block_split, RING)
            nc.vector.sem_inc(x_ready, 1)
            vec.wait_ge(tables_loaded, 32)
            for k in range(KT):
                if k in (0, 1, 2):
                    vec.wait_ge(block_hi, k + 1)
                    nc.vector.tensor_tensor(w_lo[:, k], raw[:, k], w_hi[:, k], ALU.subtract)\
                        .then_inc(block_split, 1)
                h_low(k + 1, k, 0)
            with vec.Fori(0, DEPTH) as l:
                ffn(l, 0)
                for e in range(len(MIX_STEPS)):
                    mix_step(l, e)
                for k in range(34, 40):
                    split_lo(l, MIX_AT + k + AHEAD)
                update(l, 1)
                ffn(l, 1)
            assert links[0] == VECTOR_LINKS, links

        @block.tensor
        def _(pe):
            def three(dst, w, m, start, stop):
                nc.tensor.matmul(dst, w[0], m[0], start=start, stop=False)
                nc.tensor.matmul(dst, w[0], m[1], start=False, stop=False)
                return nc.tensor.matmul(dst, w[1], m[0], start=False, stop=stop)

            def w_part(slot, a, b):
                return w_hi[:, slot, a:b], w_lo[:, slot, a:b]

            def h_part(k, a=0, b=SEQ):
                return h_hi[:, k, a:b], h_lo[:, k, a:b]

            def have_block(l, k):
                pe.wait_ge(block_split, n_block(l, k + 1) + RING)

            def first_tiles(l, s, k, dsts):
                for j in range(3):
                    have_block(l, k + j)
                for t in range(KT):
                    pe.wait_ge(h_ready, n_tile(l, s, t + 1))
                    for j, dst in enumerate(dsts):
                        ins = three(dst, w_part((k + j) % RING, t * P, (t + 1) * P), h_part(t), t == 0, t == KT - 1)
                        if t == KT - 1:
                            used(ins)

            def column_tile(l, k, dst, spread_of=None):
                have_block(l, k)
                slot = k % RING
                for t in range(KT):
                    ins = three(dst, w_part(slot, t * P, (t + 1) * P), h_part(t), t == 0, t == KT - 1)
                    if t == 5 and spread_of is not None:
                        spread(l, spread_of, 0)
                return ins

            def columns(l, s, post):
                pe.wait_ge(summed, n_summed(l, s, post, 6))
                pe.wait_ge(square_ready, n_square(l, s, post, KT))
                dst = bank[2 if post else 4]
                for t in range(NT):
                    nc.tensor.matmul(dst[:, t:t + 1], hid[:, t * P:(t + 1) * P], ones[:, 0:1],
                                     start=True, stop=False)
                    ins = nc.tensor.matmul(dst[:, t:t + 1], T[3][:, t * P:(t + 1) * P], ones[:, 0:1],
                                           start=False, stop=True)
                ins.then_inc(cols_ready, 1)

            def spread(l, s, post):
                pe.wait_ge(diag_ready, n_norm(l, s, post) + 1)
                nc.tensor.matmul(bank[3 if post else 5][:], ones[:], T[0][:], start=True, stop=True)\
                    .then_inc(scale_ready, 1)
                if post:
                    nc.tensor.matmul(bank[1][:], ones[:], T[0][:], start=True, stop=True)\
                        .then_inc(scale_twin, 1)

            def used(ins):
                ins.then_inc(block_used, 1)

            def ffn(l, part):
                k0 = FFN_AT[part]
                s = 2 * part
                first_tiles(l, s, k0, [bank[b][:] for b in range(3)])
                columns(l, s, 0)
                used(column_tile(l, k0 + 3, bank[3][:], s))
                with pe.Fori(0, UP_BLOCKS // RING - 1) as i:
                    for b in range(RING):
                        f, up = b // 2, b % 2
                        pe.wait_ge(bank_scaled, l * (4 * FT) + i * 4 + (2 * FT * part + b + 1))
                        pe.wait_ge(block_split, l * LAYER_BLOCKS + i * RING + (k0 + RING + b + 1 + RING))
                        slot = (k0 + b) % RING
                        dst = bank[2 * f + up][:]
                        for t in range(KT):
                            ins = three(dst, w_part(slot, t * P, (t + 1) * P), h_part(t), t == 0, t == KT - 1)
                        used(ins)
                for half in (0, 1):
                    k1 = k0 + UP_BLOCKS + half * DOWN_BLOCKS
                    down_block(l, s, k1, 0, half, True, False, hidden_pair, n_hidden(l, part, 2))
                    with pe.Fori(0, 2) as i:
                        for b in range(RING):
                            j = k1 + 1 + b
                            pe.wait_ge(block_split, l * LAYER_BLOCKS + i * RING + (j + 1 + RING))
                            if half == 0:
                                pe.wait_ge(hidden_split, l * (2 * FT) + i * (2 * RING) + (FT * part + 2 * b + 4))
                            for d in range(4):
                                for t in range(2):
                                    f_at = i * (2 * RING) + (2 * b + 2 + t)
                                    ins = three(bank[4 + d][:],
                                                w_part(j % RING, t * 512 + d * P, t * 512 + (d + 1) * P),
                                                (a_hi[:, f_at], a_lo[:, f_at]), False, False)
                            used(ins)
                    down_block(l, s, k1 + 9, 9, half, False, False, hidden_pair, n_hidden(l, part, 20))
                    down_block(l, s, k1 + 10, 10, half, False, True, hidden_pair, n_hidden(l, part, 22))
                columns(l, s, 1)
                spread(l, s, 1)

            def hidden_pair(f):
                return a_hi[:, f], a_lo[:, f]

            def down_block(l, s, k, j, half, first, last, pair, split_count):
                have_block(l, k)
                if split_count is not None and half == 0:
                    pe.wait_ge(hidden_split, split_count)
                slot = k % RING
                for d in range(4):
                    if first and half == 1:
                        pe.wait_ge(square_ready, n_square(l, s, 1, d + 1))
                    for t in range(2):
                        ins = three(bank[4 + d][:], w_part(slot, t * 512 + d * P, t * 512 + (d + 1) * P),
                                    pair(2 * j + t), first and t == 0, last and t == 1)
                    if last and d < 3:
                        ins.then_inc(y_done, 1)
                used(ins)

            def mix_step(l, e):
                kind, n, blks, m = MIX_STEPS[e]
                first = bank_set(kind, n) if kind != "cat_a" else 0
                slots = [(MIX_AT + k) % RING for k in blks]

                def free(b):
                    prev = last_in_bank(e, b)
                    if prev is not None:
                        pe.wait_ge(result_read, l * RESULTS + (prev + 1))

                if kind in ("z", "u", "g1", "g2"):
                    if kind == "z" and n < 3:
                        if n == 0:
                            first_tiles(l, 1, MIX_AT, [bank[b][:] for b in range(3)])
                            columns(l, 1, 0)
                        return
                    free(first + n)
                    used(column_tile(l, MIX_AT + blks[0], bank[first + n][:], 1 if kind == "z" else None))
                elif kind == "v":
                    for j, k in enumerate(blks):
                        have_block(l, MIX_AT + k)
                        if j == 0:
                            pe.wait_ge(result_read, l * RESULTS + 1)
                        for t in range(NT):
                            for kk in range(2):
                                hp = h_part(2 * j + kk, t * P, (t + 1) * P)
                                ins = three(bank[4 + t][:], hp, w_part(slots[j], kk * 512, (kk + 1) * 512),
                                            j == 0 and kk == 0, j == 3 and kk == 1)
                            if j == 3 and t < 3:
                                ins.then_inc(result, 1)
                        used(ins)
                        if j < 3:
                            if j == 0:
                                pe.wait_ge(pack_loaded, (l + 1) * 16)
                                rhs = pk[0:64, PK_Z:PK_Z + SEQ]
                            else:
                                pe.wait_ge(mlp_sin, l * 3 + j)
                                rhs = T[2][0:64, :]
                            free(j)
                            nc.tensor.matmul(bank[j][:], pk[0:64, PK_W + P * j:PK_W + P * (j + 1)], rhs,
                                             start=True, stop=True).then_inc(mlp_done, 1)
                elif kind in ("filter_sum", "filter_diff"):
                    pe.wait_ge(filt_loaded, l * 32 + 16 * (n + 1))
                    pe.wait_ge(hid_ready, l + 1)
                    if kind == "filter_diff":
                        pe.wait_ge(negated, l * 2 + (n + 1))
                    elif n:
                        pe.wait_ge(skip_loaded, (l + 1) * 16)
                    for j in range(4):
                        free(first + j)
                        with_skip = j == 0 and kind == "filter_sum"
                        ins = nc.tensor.matmul(bank[first + j][:], hid[:, j * P:(j + 1) * P], wo[:],
                                               start=True, stop=not with_skip)
                        if with_skip:
                            skip = scale_b[0:1, :] if n else pk[0:1, PK_SKIP:PK_SKIP + D_B]
                            ins = nc.tensor.matmul(bank[first][:], ident[0:1, :], skip, start=False, stop=True)
                        ins.then_inc(result, 1)
                elif kind == "fold":
                    for j in range(4):
                        free(first + j)
                    for c in range(4):
                        pe.wait_ge(fold_ready, l * 8 + (4 * n + c + 1))
                        for q in range(4):
                            ins = nc.tensor.transpose(bank[first + q][:, c * P:(c + 1) * P],
                                                      T[2 + c % 2][:, q * P:(q + 1) * P], ident[:])
                        ins.then_inc(fold_turned, 1)
                elif kind == "gmlp":
                    for c in range(4):
                        free(first + c)
                        for t in range(NT):
                            if c == 0:
                                pe.wait_ge(ln_ready, l * NT + (t + 1))
                            for side in (0, 1):
                                hd = 2 * c + side
                                ins = nc.tensor.matmul(
                                    bank[first + c][64 * side:64 * side + 64, t * P:(t + 1) * P],
                                    v[:, t, hd * HEAD_DIM:(hd + 1) * HEAD_DIM],
                                    pk[:, PK_WS + hd * P:PK_WS + (hd + 1) * P], start=True, stop=True)
                        ins.then_inc(result, 1)
                elif kind in ("kernel_cos", "kernel_sin"):
                    sin = kind == "kernel_sin"
                    have_block(l, MIX_AT + blks[0])
                    pe.wait_ge(filter_split, l * 16 + (8 * n + 4 + 4 * sin))
                    for parity in (0, 1):
                        for i in (0, 1):
                            free(first + 2 * parity + i)
                            for t in (0, 1):
                                j = 2 * parity + t
                                ins = three(bank[first + 2 * parity + i][:],
                                            w_part(slots[0], j * 256 + i * P, j * 256 + (i + 1) * P),
                                            (s_hi[:, 4 * sin + j], s_lo[:, 4 * sin + j]), t == 0, t == 1)
                    used(ins)
                elif kind in ("forward_low", "forward_high"):
                    have_block(l, MIX_AT + blks[0])
                    fold_e = MIX_STEPS.index(("fold", n, (), 4))
                    pe.wait_ge(result_read, n_read(l, fold_e, 4))
                    for s in (0, 1):
                        for i in (0, 1):
                            free(first + 2 * s + i)
                            for t in (0, 1):
                                a = t * 512 + s * 256 + i * P
                                ins = three(bank[first + 2 * s + i][:], w_part(slots[0], a, a + P),
                                            (fold_hi[:, 2 * s + t], fold_lo[:, 2 * s + t]), t == 0, t == 1)
                    used(ins)
                elif kind == "inverse":
                    pe.wait_ge(spectrum_split, l * 16 + (8 * n + 8))
                    for side, k in enumerate(blks):
                        have_block(l, MIX_AT + k)
                        for c in range(4):
                            if side == 0:
                                free(first + c)
                            for q in range(4):
                                j = 4 * side + q
                                ins = three(bank[first + c][:, side * HALF_SEQ:(side + 1) * HALF_SEQ],
                                            (s_hi[:, j, c * P:(c + 1) * P], s_lo[:, j, c * P:(c + 1) * P]),
                                            w_part(slots[side], q * 256, (q + 1) * 256), q == 0, q == 3)
                            if side == 1 and c < 3:
                                ins.then_inc(result, 1)
                        used(ins)
                elif kind == "out_a":
                    for b in range(4, 8):
                        free(b)
                    pe.wait_ge(cat_split, l * 8 + 4)
                    for j in (0, 1):
                        down_block(l, 1, MIX_AT + 30 + j, j, 0, j == 0, False, h_part, None)

            pe.sem_inc(block_used, RING)
            pe.sem_inc(cols_ready, 1)
            pe.wait_ge(tables_loaded, 32)
            with pe.Fori(0, DEPTH) as l:
                ffn(l, 0)
                for e in range(len(MIX_STEPS)):
                    mix_step(l, e)
                pe.wait_ge(cat_split, l * 8 + 8)
                for j in (2, 3):
                    down_block(l, 1, MIX_AT + 32 + j, j, 0, False, j == 3, h_part, None)
                for j in range(4):
                    down_block(l, 1, MIX_AT + 36 + j, j, 1, j == 0, j == 3, h_part, None)
                columns(l, 1, 1)
                spread(l, 1, 1)
                ffn(l, 1)



def transform_tables():
    f_low = np.arange(256)
    freq = np.concatenate([f_low, 511 - f_low])
    lag = np.concatenate([np.arange(0, SEQ, 2), np.arange(1, SEQ, 2)])
    kern = np.pi * np.outer(lag, 2 * f_low + 1) / 1024
    time = np.pi * np.outer(np.arange(256) + 0.5, 2 * freq + 1) / 1024
    blk = lambda a, n: a.astype(np.float32).reshape(n, P, BLOCK // n).transpose(1, 0, 2).reshape(P, BLOCK)
    kernel_cos, kernel_sin = blk(np.cos(kern), 4), blk(-np.sin(kern), 4)
    low = blk(np.concatenate([np.cos(time[:, :256]), -np.sin(time[:, :256])], 1), 2)
    high = blk(np.concatenate([np.cos(time[:, 256:]), -np.sin(time[:, 256:])], 1), 2)
    inv_cos, inv_sin = blk(np.cos(time).T / 512, 4), blk(np.sin(time).T / 512, 4)
    return kernel_cos, kernel_sin, low, high, inv_cos, inv_sin, lag


def filter_tables(lag):
    f32 = np.float32
    t = np.linspace(0.0, 1.0, SEQ, dtype=f32)
    bands = np.linspace(1e-4, 15, 16, dtype=f32)
    ang = f32(2.0 * np.pi / SEQ) * np.arange(SEQ, dtype=f32)[:, None] * bands[None, :]
    z = np.zeros((64, SEQ), f32)
    z[:FILTER_EMB] = np.concatenate([t[:, None], np.cos(ang), -np.sin(ang)], -1)[lag].T
    low, high = np.log(1e-2) / 1.5, np.log(1e-2) / 0.3
    deltas = np.abs(np.linspace(low, high, D_B, dtype=f32))
    decay = np.exp(-t[lag][:, None] * deltas).astype(f32)
    return z, decay.reshape(4, P, D_B).transpose(1, 0, 2)



def kernel(**inputs):
    import concourse.bacc as _bacc
    from concourse.bass_utils import run_bass_kernel_spmd as _run

    a = {k: np.asarray(w) for k, w in inputs.items()}
    L = DEPTH
    kc, ks, fl, fh, ic, is_, lag = transform_tables()
    z, decay = filter_tables(lag)

    def column_blocks(w):
        n = w.shape[1] // P
        return w.reshape(KT, P, n, P).transpose(2, 1, 0, 3).reshape(n, P, BLOCK)

    def row_blocks(w):
        n = w.shape[0] // (2 * P)
        return w.reshape(n, 2, P, 512).transpose(0, 2, 1, 3).reshape(n, P, BLOCK)

    stream = np.zeros((L * LAYER_BLOCKS + PADDING, P, BLOCK), np.float32)
    blocks = stream[:L * LAYER_BLOCKS].reshape(L, LAYER_BLOCKS, P, BLOCK)
    for l in range(L):
        for part in (0, 1):
            k0 = part * (FFN_BLOCKS + MIX_BLOCKS)
            name = f"ffn{part + 1}_w_"
            blocks[l, k0:k0 + UP_BLOCKS:2] = column_blocks(a[name + "gate"][l])
            blocks[l, k0 + 1:k0 + UP_BLOCKS:2] = column_blocks(a[name + "up"][l])
            for half in (0, 1):
                k1 = k0 + UP_BLOCKS + half * DOWN_BLOCKS
                blocks[l, k1:k1 + DOWN_BLOCKS] = row_blocks(a[name + "down"][l][:, half * 512:half * 512 + 512])
        w, mix = a["mix_w_in"][l], blocks[l, FFN_BLOCKS:FFN_BLOCKS + MIX_BLOCKS]
        mix[0:4] = column_blocks(w[:, 1024:1536])
        mix[4:8] = row_blocks(w[:, 512:1024])
        mix[8:12] = column_blocks(w[:, 0:512])
        mix[14:18] = column_blocks(w[:, 1536:2048])
        mix[20:24] = column_blocks(w[:, 2048:2560])
        for at in (12, 26):
            mix[at], mix[at + 1] = kc, ks
        for at in (18, 28):
            mix[at], mix[at + 1] = fl, fh
        for at in (24, 32):
            mix[at], mix[at + 1] = ic, is_
        w = a["mix_w_out"][l]
        first, second = row_blocks(w[:, 0:512]), row_blocks(w[:, 512:1024])
        mix[30:32], mix[34:36], mix[36:40] = first[0:2], first[2:4], second

    params = np.empty((L, PARAMS, P), np.float32)
    for l in range(L):
        for i, name in enumerate(("ffn1_pre_g", "ffn1_post_g", "mix_pre_g", "mix_post_g",
                                  "ffn2_pre_g", "ffn2_post_g")):
            params[l, 8 * i:8 * i + 8] = a[name][l].reshape(KT, P)
        params[l, CONV_W:CONV_W + 36] = a["hy_conv_w"][l].reshape(36, P)
        params[l, CONV_B:CONV_B + 12] = a["hy_conv_b"][l].reshape(12, P)
        for i, name in enumerate(("b1", "b2", "b3", "freq")):
            params[l, FILT_B + i] = np.tile(a["hy_filt_" + name][l], 2)
        params[l, NEXT_PRE:NEXT_PRE + 8] = a["ffn1_pre_g"][min(l + 1, L - 1)].reshape(KT, P)

    pack = np.zeros((L, P, PACK), np.float32)
    filt_out = np.empty((L, 2, P, D_B), np.float32)
    for l in range(L):
        pack[l, :, PK_WS:PK_WS + 1024] = a["gmlp_w_s"][l].transpose(2, 0, 1).reshape(P, HEADS * P)
        pack[l, :, PK_LNG:PK_LNG + 512] = a["gmlp_ln_g"][l]
        pack[l, :, PK_LNB:PK_LNB + 512] = a["gmlp_ln_b"][l]
        bias = a["gmlp_b_s"][l].reshape(4, 2, 1, P)
        pack[l, :, PK_BS:PK_BS + 512] = np.broadcast_to(bias, (4, 2, HEAD_DIM, P)).transpose(1, 2, 0, 3).reshape(P, 512)
        for i in (1, 2, 3):
            w = a[f"hy_filt_w{i}"][l]
            for side in (0, 64):
                at = PK_W + P * (i - 1) + side
                pack[l, 0:w.shape[0], at:at + 64] = w
        pack[l, 0:64, PK_Z:PK_Z + SEQ] = z
        pack[l, 0, PK_SKIP:PK_SKIP + D_B] = a["hy_skip"][l, 0]
        w = a["hy_filt_w_out"][l].reshape(64, 2, 2, D_B)
        filt_out[l] = w.transpose(1, 2, 0, 3).reshape(2, P, D_B)

    x_t = a["x"][0].T.reshape(KT, P, SEQ).transpose(1, 0, 2)
    arrays = {
        "blocks": stream,
        "x_in": x_t,
        "params": params.transpose(0, 2, 1),
        "pack": pack,
        "filt_out": filt_out.reshape(2 * L, P, D_B),
        "skip1": a["hy_skip"][:, 1:2],
        "decay": decay,
        "squares": np.stack([np.eye(P, dtype=np.float32), np.ones((P, P), np.float32)]),
    }
    arrays = {k: np.ascontiguousarray(w) for k, w in arrays.items()}
    nc = _bacc.Bacc("TRN2", target_bir_lowering=False, num_devices=1)
    args = [nc.dram_tensor(k, w.shape, F32, kind="ExternalInput").ap() for k, w in arrays.items()]
    out = nc.dram_tensor("out_t", (P, KT, SEQ), F32, kind="ExternalOutput").ap()
    build_encoder(nc, *args, out)
    r = _run(nc, [arrays], core_ids=[0])
    y = r.results[0]["out_t"]
    return np.ascontiguousarray(y.transpose(1, 0, 2).reshape(D_MODEL, SEQ).T).reshape(1, SEQ, D_MODEL)
```

```python
from contextlib import ExitStack

import numpy as np
import concourse.bass as bass
from concourse import mybir

F32 = mybir.dt.float32
F32R = mybir.dt.float32r
I32 = mybir.dt.int32
ALU = mybir.AluOpType
ACT = mybir.ActivationFunctionType

P = 128
SEQ = 512
D_MODEL = 1024
D_FF = 2816
D_B = 512
HEADS = 8
HEAD_DIM = 64
DEPTH = 2
FILTER_EMB = 33
RMS_EPS = 1e-6
LN_EPS = 1e-5

KT = D_MODEL // P
FT = D_FF // P
NT = SEQ // P
HALF_SEQ = SEQ // 2

BLOCK = 1024
UP_BLOCKS = 2 * FT
DOWN_BLOCKS = FT // 2
FFN_BLOCKS = UP_BLOCKS + 2 * DOWN_BLOCKS
MIX_BLOCKS = 40
LAYER_BLOCKS = 2 * FFN_BLOCKS + MIX_BLOCKS
FFN_AT = (0, FFN_BLOCKS + MIX_BLOCKS)
MIX_AT = FFN_BLOCKS
RING = 4
AHEAD = 3
PADDING = RING
assert LAYER_BLOCKS % RING == 0 and UP_BLOCKS % RING == 0 and DOWN_BLOCKS == 11

PRE = (0, 16, 32)
CONV_W = 48
CONV_B = 84
FILT_B = 96
NEXT_PRE = 100
PARAMS = 108

PK_WS = 0
PK_LNG = 1024
PK_LNB = 1536
PK_BS = 2048
PK_W = 2560
PK_Z = 2944
PK_SKIP = 3456
PACK = 3968

ROUND = 1.5 * 2.0 ** 23
PI_BELOW = 3.1415925
TWO_PI = 6.283185307179586

MIX_PLAN = [
    ("z", 0, 1, 1, 0), ("z", 1, 1, 1, 0), ("z", 2, 1, 1, 0), ("z", 3, 1, 1, 0),
    ("mlp", 0, 0, 0, 0), ("v", 0, 4, 4, 4),
    ("u", 0, 1, 1, 0), ("filter_sum", 0, 0, 4, 4), ("u", 1, 1, 1, 0), ("filter_diff", 0, 0, 4, 4),
    ("diff_low", 0, 0, 0, 0),
    ("u", 2, 1, 1, 0), ("fold_parts", 0, 0, 0, 0), ("gmlp", 0, 0, 4, 4), ("u", 3, 1, 1, 0),
    ("gmlp_gate", 0, 0, 0, 0),
    ("fold", 0, 0, 4, 0), ("kernel_cos", 0, 1, 4, 4), ("g1", 0, 1, 1, 0),
    ("kernel_sin", 0, 1, 4, 4), ("g1", 1, 1, 1, 0),
    ("forward_low", 0, 1, 4, 4), ("g1", 2, 1, 1, 0), ("forward_high", 0, 1, 4, 4),
    ("g1", 3, 1, 1, 0), ("g2", 0, 1, 1, 0),
    ("inverse", 0, 2, 4, 4), ("filter_sum", 1, 0, 4, 0), ("fold_parts", 1, 0, 0, 0),
    ("g2", 1, 1, 1, 4), ("filter_diff", 1, 0, 4, 0), ("g2", 2, 1, 1, 5),
    ("fold", 1, 0, 4, 4), ("diff_low", 1, 0, 0, 0), ("kernel_cos", 1, 1, 4, 0), ("g2", 3, 1, 1, 4),
    ("cat_a", 0, 0, 0, 0), ("kernel_sin", 1, 1, 4, 4),
    ("forward_low", 1, 1, 4, 0), ("out_a", 0, 1, 0, 4), ("forward_high", 1, 1, 4, 0),
    ("out_a", 1, 1, 0, 4),
    ("inverse", 1, 2, 4, 0),
]
MIX_STEPS = []
for _kind, _n, _count, _results, _bank in MIX_PLAN:
    _at = sum(len(step[2]) for step in MIX_STEPS)
    MIX_STEPS.append((_kind, _n, tuple(range(_at, _at + _count)), _results, _bank))
STEP_AT = {step[:2]: e for e, step in enumerate(MIX_STEPS)}
OUT_AT = sum(len(step[2]) for step in MIX_STEPS)
assert OUT_AT + 6 == MIX_BLOCKS
RESULTS = sum(s[3] for s in MIX_STEPS)
SIGNALLED = {"v": 3, "filter_sum": 4, "filter_diff": 4, "gmlp": 4, "inverse": 3}
STAGED = {"z": 1, "g1": 1, "g2": 1, "u": 1, "v": 4, "filter_sum": 4, "filter_diff": 4, "fold": 4,
          "kernel_cos": 2, "kernel_sin": 2, "forward_low": 4, "forward_high": 4, "inverse": 4}
MLP_IN_V = {5: 1, 6: 2}
assert STEP_AT[("v", 0)] == 5 and MIX_STEPS[5][2] == (4, 5, 6, 7)
VECTOR_LINKS = 116


def build_encoder(nc, blocks, xt, params, pack, filt_out, skip1, decay, identity, out):
    base = (nc.sbuf_base + 31) // 32 * 32
    place = [base]

    def sb(name, shape, dt=F32, at=None):
        size = 4 * int(np.prod(shape[1:]))
        if at is None:
            at = place[0]
            place[0] += (size + 31) // 32 * 32
        return nc.alloc_sbuf_tensor_at(name, shape, dt, offset=at)

    x = sb("x_t", [P, KT, SEQ])
    h_hi = sb("h_hi", [P, KT, SEQ], F32R)
    h_lo = sb("h_lo", [P, KT, SEQ], F32R)
    y_at = place[0]
    y = sb("y_first_half", [P, 4, SEQ])
    decay_sb = sb("decay_table", [P, 4, SEQ], at=y_at)
    raw = sb("raw_blocks", [P, RING, BLOCK])
    w_hi = sb("block_hi", [P, RING, BLOCK], F32R)
    w_lo = sb("block_lo", [P, RING, BLOCK], F32R)
    act_at = place[0]
    a_hi = sb("hidden_hi", [P, FT, SEQ], F32R)
    a_lo = sb("hidden_lo", [P, FT, SEQ], F32R)
    assert place[0] - act_at == 44 * 2048
    tile = lambda n: act_at + 2048 * n
    zg2 = sb("z_then_gate2", [P, 4, SEQ], at=tile(0))
    g1 = sb("gate1_then_z1", [P, 4, SEQ], at=tile(4))
    u = sb("gmlp_u", [P, 4, SEQ], at=tile(8))
    v = sb("gmlp_v", [P, NT, SEQ], at=tile(12))
    fold_lo = sb("fold_lo", [P, 4, SEQ], F32R, at=tile(12))
    k_spec = sb("kernel_spectrum", [P, 8, SEQ], at=tile(16))
    pk = sb("mixer_pack", [P, PACK], at=tile(16))
    to_split = sb("filter_or_spectrum", [P, 8, SEQ], at=tile(32))
    fold_src = sb("fold_parts", [P, 4, SEQ], at=tile(40))
    skip_row = sb("skip_second_order", [P, SEQ], at=tile(12))
    s_hi = sb("filter_or_spectrum_hi", [P, 8, SEQ], F32R, at=tile(24))
    s_lo = sb("filter_or_spectrum_lo", [P, 8, SEQ], F32R, at=tile(32))
    fold_hi = sb("fold_hi", [P, 4, SEQ], F32R, at=tile(40))
    scale_b = sb("rms_scale", [P, SEQ])
    T = [sb(f"work{i}", [P, SEQ]) for i in range(4)]
    hid = sb("square_sum_or_filter_hidden", [P, SEQ])
    wo = sb("filter_out_weights", [P, D_B])
    ident = sb("identity", [P, P])
    unread = sb("unread", [P, 1])
    ones = sb("ones", [P, P])
    unit = sb("ones_by_column", [P, NT, NT])
    par = sb("layer_params", [P, PARAMS])
    mean_sq = sb("mean_square", [P, NT])
    newton = sb("newton_term", [P, NT])
    rcol = sb("rms_scale_columns", [P, NT])
    stats = sb("ln_stats", [P, NT, 6])
    mv = sb("ln_mean_var", [P, NT, 2])
    rstd = sb("ln_rstd", [P, NT])
    assert place[0] <= nc.sbuf_usable_end, (place[0], nc.sbuf_usable_end)

    with ExitStack() as ctx:
        bank = [ctx.enter_context(nc.psum_tensor(f"bank{i}", [P, SEQ], F32)) for i in range(8)]

        def sem(name):
            return ctx.enter_context(nc.semaphore(name))

        landed = [sem(f"block_landed{i}") for i in range(RING)]
        x_loaded = [sem(f"x_loaded{i}") for i in range(4)]
        tables_loaded = sem("tables_loaded")
        ones_ready = sem("ones_ready")
        params_loaded = sem("params_loaded")
        pack_loaded = sem("pack_loaded")
        filt_loaded = sem("filter_out_loaded")
        skip_loaded = sem("skip_loaded")
        decay_loaded = sem("decay_loaded")
        stored = sem("out_stored")
        block_hi = sem("block_hi_ready")
        block_split = sem("block_split")
        block_used = sem("block_used")
        x_ready = sem("x_updated")
        y_scaled = sem("y_scaled")
        h_hi_ready = sem("h_hi_ready")
        h_ready = sem("h_split")
        square_ready = sem("square_ready")
        summed = sem("squares_summed")
        cols_ready = sem("mean_square_columns")
        diag_ready = sem("scale_diagonal")
        scale_ready = sem("scale_broadcast")
        scale_twin = sem("scale_broadcast_twin")
        scale_copied = sem("scale_in_sbuf")
        bank_scaled = sem("gate_up_scaled")
        silu_ready = sem("silu_ready")
        hidden_ready = sem("hidden_ready")
        hidden_hi = sem("hidden_hi_ready")
        hidden_split = sem("hidden_split")
        y_done = sem("y_bank_done")
        chain = sem("vector_step")
        ln_chain = sem("pool_step")
        load_go = sem("small_load_may_start")
        stats_go = sem("ln_stats_seen")
        result = sem("mixer_result")
        result_read = sem("mixer_result_read")
        staged = sem("mixer_result_staged")
        mlp_done = sem("filter_mlp_done")
        mlp_arg = sem("filter_mlp_argument")
        mlp_sin = sem("filter_mlp_sine")
        hid_ready = sem("filter_hidden_ready")
        negated = sem("filter_out_negated")
        filter_split = sem("filter_split")
        fold_ready = sem("fold_ready")
        fold_turned = sem("fold_transposed")
        product_summed = sem("spectrum_product_summed")
        spectrum_split = sem("spectrum_split")
        ln_centred = sem("ln_centred")
        ln_ready = sem("ln_ready")
        gmlp_ready = sem("gmlp_ready")
        gated = sem("hyena_gated")
        cat_hi = sem("cat_hi_ready")
        cat_split = sem("cat_split")
        block = ctx.enter_context(nc.Block())

        def n_block(l, k):
            return l * LAYER_BLOCKS + k

        def n_landed(l, k):
            return (l * (LAYER_BLOCKS // RING) + (k // RING) + 1) * 16

        def n_tile(l, s, k):
            return l * 24 + (8 * s + k)

        def n_updated(l, s, k):
            return l * 24 + (8 * s + k + 1)

        def n_columns(l, s, post):
            return l * 6 + (2 * s + post + 1)

        def n_summed(l, s, post, k):
            return l * 36 + (12 * s + 7 * post + k + 1)

        def n_square(l, s, post, k):
            return l * 48 + (16 * s + 8 * post + k)

        def n_norm(l, s, post):
            return l * 6 + (2 * s + post)

        def n_hidden(l, part, f):
            return l * (2 * FT) + (FT * part + f)

        def bases(count):
            at = [0]
            for step in MIX_STEPS:
                at.append(at[-1] + count(step))
            return at

        base_of = bases(lambda step: step[3])
        signalled_of = bases(lambda step: SIGNALLED.get(step[0], 0))
        staged_of = bases(lambda step: STAGED.get(step[0], 0))

        def n_read(l, e, i):
            return l * RESULTS + (base_of[e] + i)

        def n_staged(l, e, i):
            return l * staged_of[-1] + (staged_of[e] + i)

        def wait_block(eng, l, k):
            eng.wait_ge(block_used, n_block(l, k + 1) + RING)

        def wait_result(eng, l, e, i):
            kind, n, blks, m, _ = MIX_STEPS[e]
            if kind == "fold":
                eng.wait_ge(fold_turned, l * 2 + (n + 1))
            elif blks and (i == m or kind not in SIGNALLED):
                wait_block(eng, l, MIX_AT + blks[-1])
            else:
                eng.wait_ge(result, l * signalled_of[-1] + (signalled_of[e] + i))

        def scaled(kind, n):
            return T[n] if kind == "z" else T[n % 2]

        def n_y_done(l, s, half, d):
            return l * 18 + (6 * s + 3 * half + d)

        def last_down(s, half):
            if s == 1:
                return MIX_AT + OUT_AT + 1 + 4 * half
            return FFN_AT[s // 2] + UP_BLOCKS + (half + 1) * DOWN_BLOCKS - 1

        def last_in_bank(e, b):
            for d in range(e - 1, -1, -1):
                _, n, _, m, first = MIX_STEPS[d]
                if m == 1 and first + n == b:
                    return base_of[d]
                if m == 4 and first <= b < first + 4:
                    return base_of[d] + 3
            return None

        @block.sync
        def _(sp):
            with sp.Fori(0, (DEPTH * LAYER_BLOCKS + PADDING) // RING) as r:
                for j in range(RING):
                    sp.wait_ge(block_split, r * RING + (j + 1))
                    sp.dma_start(raw[:, j], blocks[r * RING + j]).then_inc(landed[j], 16)
            for k in range(KT):
                sp.wait_ge(x_ready, n_updated(DEPTH - 1, 2, k + 1))
                sp.dma_start(out[:, k], x[:, k]).then_inc(stored, 16)
            sp.wait_ge(stored, 16 * KT)

        @block.gpsimd
        def _(pool):
            pool.sem_inc(summed, 1)
            pool.dma_start(par[:], params[0]).then_inc(params_loaded, 16)
            pool.dma_start(ident[:], identity).then_inc(tables_loaded, 16)
            nc.gpsimd.memset(ones[:], 1.0).then_inc(ones_ready, 1)
            nc.gpsimd.memset(unit[:], 0.0).then_inc(ones_ready, 1)
            pool.wait_ge(ones_ready, 2)
            for t in range(NT):
                nc.gpsimd.memset(unit[:, t, t:t + 1], 1.0).then_inc(ones_ready, 1)

            def sum_squares(l, s, post):
                pool.wait_ge(cols_ready, n_columns(l, s, post))
                for k in range(1, KT - 2 if post else KT):
                    pool.wait_ge(square_ready, n_square(l, s, post, k + 1))
                    first = T[2][:] if k == 1 else hid[:]
                    if k > 1:
                        pool.wait_ge(summed, n_summed(l, s, post, k - 1))
                    nc.gpsimd.tensor_tensor(hid[:], first, T[2 + k % 2][:], ALU.add).then_inc(summed, 1)

            def sum_products(l, n, half):
                e = STEP_AT[("forward_" + half, n)]
                for i in (0, 1):
                    q = i + 2 * (half == "high")
                    for part, op in ((0, ALU.subtract), (1, ALU.add)):
                        pool.wait_ge(result_read, n_read(l, e, 2 * i + part + 1))
                        nc.gpsimd.tensor_tensor(to_split[:, 4 * part + q], to_split[:, 4 * part + q],
                                                T[2 * i + part][:], op).then_inc(product_summed, 1)

            for k in range(1, KT):
                pool.wait_ge(square_ready, k + 1)
                if k > 1:
                    pool.wait_ge(summed, k)
                nc.gpsimd.tensor_tensor(hid[:], T[2][:] if k == 1 else hid[:], T[2 + k % 2][:], ALU.add)\
                    .then_inc(summed, 1)
            with pool.Fori(0, DEPTH) as l:
                pool.wait_ge(h_ready, n_tile(l, 0, 8))
                pool.sem_inc(load_go, 1)
                pool.dma_start(par[:], params[l]).then_inc(params_loaded, 16)
                sum_squares(l, 0, 1)
                wait_block(pool, l, last_down(0, 1))
                pool.sem_inc(load_go, 1)
                pool.dma_start(pk[:], pack[l]).then_inc(pack_loaded, 16)
                pool.dma_start(wo[:], filt_out[l * 2]).then_inc(filt_loaded, 16)
                sum_squares(l, 1, 0)
                pool.wait_ge(x_ready, n_updated(l, 0, 8))
                pool.sem_inc(load_go, 1)
                pool.dma_start(decay_sb[:], decay).then_inc(decay_loaded, 16)
                pool.wait_ge(pack_loaded, (l + 1) * 16)
                for t in range(NT):
                    pool.wait_ge(ln_centred, l * NT + (t + 1))
                    nc.gpsimd.tensor_tensor(v[:, t], v[:, t], pk[:, PK_LNG:PK_LNG + 512], ALU.mult)\
                        .then_inc(ln_chain, 1)
                    pool.wait_ge(ln_chain, l * NT + (t + 1))
                    nc.gpsimd.tensor_tensor(v[:, t], v[:, t], pk[:, PK_LNB:PK_LNB + 512], ALU.add)\
                        .then_inc(ln_ready, 1)
                wait_result(pool, l, STEP_AT[("filter_diff", 0)], 4)
                pool.sem_inc(load_go, 1)
                pool.dma_start(wo[:], filt_out[l * 2 + 1]).then_inc(filt_loaded, 16)
                sum_products(l, 0, "low")
                sum_products(l, 0, "high")
                wait_result(pool, l, STEP_AT[("forward_high", 0)], 4)
                pool.sem_inc(load_go, 1)
                pool.dma_start(skip_row[0:1, :], skip1[l]).then_inc(skip_loaded, 16)
                for c in range(4):
                    pool.wait_ge(cat_hi, l * 8 + (c + 1))
                    nc.gpsimd.tensor_tensor(h_lo[:, c], u[:, c], h_hi[:, c], ALU.subtract).then_inc(cat_split, 1)
                sum_products(l, 1, "low")
                sum_products(l, 1, "high")
                sum_squares(l, 1, 1)
                sum_squares(l, 2, 0)
                sum_squares(l, 2, 1)
                sum_squares(l + 1, 0, 0)

        @block.scalar
        def _(act):
            def split_hi(l, k):
                slot = k % RING
                act.wait_ge(landed[slot], n_landed(l, k))
                act.wait_ge(block_used, n_block(l, k + 1))
                nc.scalar.activation(w_hi[:, slot], raw[:, slot], ACT.Copy).then_inc(block_hi, 1)

            def square_tile(l, s, post, k, src):
                if k < 2:
                    act.wait_ge(cols_ready, n_columns(l, s, post))
                else:
                    act.wait_ge(summed, n_summed(l, s, post, max(k - 2, 1)))
                nc.scalar.activation(T[2 + k % 2][:], src, ACT.Square).then_inc(square_ready, 1)

            def before(l, s, gain):
                after = (l, s + 1) if s < 2 else (l + 1, 0)
                for k in range(KT):
                    if k == 1:
                        act.wait_ge(scale_twin, l * 3 + (s + 1))
                        nc.scalar.activation(scale_b[:], bank[2][:], ACT.Copy).then_inc(scale_copied, 1)
                    act.wait_ge(x_ready, n_updated(l, s, k + 1))
                    nc.scalar.activation(h_hi[:, k], x[:, k], ACT.Copy,
                                         scale=par[:, gain + k:gain + k + 1]).then_inc(h_hi_ready, 1)
                    square_tile(*after, 0, k, x[:, k])

            def after_half(l, s, half):
                for d in range(4):
                    k = 4 * half + d
                    if d < 3:
                        act.wait_ge(y_done, n_y_done(l, s, half, d + 1))
                    else:
                        wait_block(act, l, last_down(s, half))
                    if half == 0:
                        nc.scalar.activation(y[:, d], bank[4 + d][:], ACT.Copy)
                    square_tile(l, s, 1, k, bank[4 + d][:])

            def hidden(l, part, f):
                act.wait_ge(bank_scaled, n_hidden(l, part, f) * 2 + 1)
                nc.scalar.activation(T[1][:], T[0][:], ACT.Silu).then_inc(silu_ready, 1)
                act.wait_ge(hidden_ready, n_hidden(l, part, f) + 1)
                nc.scalar.activation(a_hi[:, f], T[3][:], ACT.Copy).then_inc(hidden_hi, 1)

            def ffn(l, part):
                k0 = FFN_AT[part]
                s = 2 * part
                for f in (0, 1):
                    split_hi(l, k0 + 2 * f + AHEAD)
                    split_hi(l, k0 + 2 * f + 1 + AHEAD)
                    hidden(l, part, f)
                with act.Fori(0, UP_BLOCKS // RING - 1) as i:
                    for f in (2, 3):
                        for b in (0, 1):
                            j = k0 + 2 * f + b + AHEAD
                            act.wait_ge(landed[j % RING],
                                        (l * (LAYER_BLOCKS // RING) + i + (j // RING + 1)) * 16)
                            act.wait_ge(block_used, l * LAYER_BLOCKS + i * RING + (j + 1))
                            nc.scalar.activation(w_hi[:, j % RING], raw[:, j % RING], ACT.Copy)\
                                .then_inc(block_hi, 1)
                        n = l * (2 * FT) + i * 2 + (FT * part + f)
                        act.wait_ge(bank_scaled, n * 2 + 1)
                        nc.scalar.activation(T[1][:], T[0][:], ACT.Silu).then_inc(silu_ready, 1)
                        act.wait_ge(hidden_ready, n + 1)
                        nc.scalar.activation(a_hi[:, i * 2 + f], T[3][:], ACT.Copy).then_inc(hidden_hi, 1)
                for half in (0, 1):
                    down(l, s, k0 + UP_BLOCKS + half * DOWN_BLOCKS, half)

            def down(l, s, k1, half):
                split_hi(l, k1 + AHEAD)
                with act.Fori(0, 2) as i:
                    for b in range(RING):
                        j = k1 + 1 + b + AHEAD
                        act.wait_ge(landed[j % RING],
                                    (l * (LAYER_BLOCKS // RING) + i + (j // RING + 1)) * 16)
                        act.wait_ge(block_used, l * LAYER_BLOCKS + i * RING + (j + 1))
                        nc.scalar.activation(w_hi[:, j % RING], raw[:, j % RING], ACT.Copy)\
                            .then_inc(block_hi, 1)
                for b in (9, 10):
                    split_hi(l, k1 + b + AHEAD)
                after_half(l, s, half)

            def mlp_sine(l, m):
                act.wait_ge(mlp_arg, l * 3 + (m + 1))
                nc.scalar.activation(hid[:] if m == 2 else T[2][:], T[0][:], ACT.Sin).then_inc(mlp_sin, 1)

            def mix_step(l, e):
                kind, n, blks, _, first = MIX_STEPS[e]
                for k in blks[:1] if kind == "inverse" else blks:
                    split_hi(l, MIX_AT + k + AHEAD)
                    if kind == "v" and k in MLP_IN_V:
                        mlp_sine(l, MLP_IN_V[k])
                if kind == "z" and n < 2:
                    pass
                elif kind == "z" and n == 2:
                    for m in (0, 1, 2):
                        middle_tap(l, e - 2 + m, kind, m)
                elif kind in ("z", "g1", "g2"):
                    middle_tap(l, e, kind, n)
                elif kind == "mlp":
                    mlp_sine(l, n)
                elif kind == "v":
                    for t in range(NT):
                        wait_result(act, l, e, t + 1)
                        nc.scalar.activation(v[:, t], bank[first + t][:], ACT.Gelu,
                                             scale=rcol[:, t:t + 1]).then_inc(staged, 1)
                elif kind == "u":
                    act.wait_ge(result_read, n_read(l, e, 1))
                    nc.scalar.activation(u[:, n], T[n % 2][:], ACT.Gelu).then_inc(staged, 1)
                elif kind in ("filter_sum", "filter_diff"):
                    for j in range(4):
                        act.wait_ge(result_read, n_read(l, e, j + 1))
                        q = j + 4 * (kind == "filter_diff")
                        nc.scalar.activation(s_hi[:, q], to_split[:, q], ACT.Copy).then_inc(staged, 1)
                elif kind == "fold":
                    for q in range(4):
                        wait_result(act, l, e, 4)
                        nc.scalar.activation(fold_hi[:, q], bank[first + q][:], ACT.Copy).then_inc(staged, 1)
                elif kind in ("kernel_cos", "kernel_sin"):
                    wait_result(act, l, e, 4)
                    before_it = STEP_AT[("forward_high", 0) if n else ("gmlp", 0)]
                    act.wait_ge(result_read, n_read(l, before_it, 4))
                    for i in (0, 1):
                        nc.scalar.activation(k_spec[:, 4 * (kind == "kernel_sin") + i], bank[first + i][:],
                                             ACT.Copy).then_inc(staged, 1)
                elif kind in ("forward_low", "forward_high"):
                    for i in (0, 1):
                        q = i + 2 * (kind == "forward_high")
                        for part in (0, 1):
                            act.wait_ge(product_summed, l * 16 + (8 * n + 2 * q + part + 1))
                            nc.scalar.activation(s_hi[:, 4 * part + q], to_split[:, 4 * part + q], ACT.Copy)\
                                .then_inc(staged, 1)
                elif kind == "inverse":
                    for c in range(4):
                        wait_result(act, l, e, c + 1)
                        if c >= 2:
                            act.wait_ge(result_read, n_read(l, e, c - 1))
                        nc.scalar.activation(T[2 + c % 2][:, 0:HALF_SEQ], bank[first + c][:, 0:HALF_SEQ],
                                             ACT.Copy).then_inc(staged, 1)
                        if n == 1 and c >= 1:
                            cat_yb(l, c - 1)
                    if n == 1:
                        cat_yb(l, 3)
                    split_hi(l, MIX_AT + blks[1] + AHEAD)
                elif kind == "cat_a":
                    wait_block(act, l, MIX_AT + MIX_STEPS[STEP_AT[("g2", 3)]][2][0])
                    for c in range(4):
                        act.wait_ge(gmlp_ready, l * 4 + (c + 1))
                        nc.scalar.activation(h_hi[:, c], u[:, c], ACT.Copy).then_inc(cat_hi, 1)

            def middle_tap(l, e, kind, n):
                c = n + {"z": 0, "g1": 4, "g2": 8}[kind]
                dst = {"z": zg2, "g1": g1, "g2": zg2}[kind]
                act.wait_ge(result_read, n_read(l, e, 1))
                nc.scalar.activation(dst[:, n], scaled(kind, n)[:], ACT.Identity,
                                     bias=par[:, CONV_B + c:CONV_B + c + 1],
                                     scale=par[:, CONV_W + 12 + c:CONV_W + 13 + c]).then_inc(staged, 1)

            def cat_yb(l, c):
                act.wait_ge(gated, l * 4 + (c + 1))
                nc.scalar.activation(h_hi[:, 4 + c], zg2[:, c], ACT.Copy).then_inc(cat_hi, 1)

            def load_x(i):
                act.dma_start(x[:, 2 * i:2 * i + 2], xt[:, 2 * i:2 * i + 2]).then_inc(x_loaded[i], 16)

            def first_block_hi(k):
                act.wait_ge(landed[k], 16)
                nc.scalar.activation(w_hi[:, k], raw[:, k], ACT.Copy).then_inc(block_hi, 1)

            load_x(0)
            act.wait_ge(ones_ready, 1)
            nc.scalar.activation(unread[:], ones[:, 0:1], ACT.Copy)
            first_block_hi(0)
            for i in (1, 2, 3):
                load_x(i)
            act.wait_ge(params_loaded, 16)
            for k in range(KT):
                if k % 2 == 0:
                    act.wait_ge(x_loaded[k // 2], 16)
                nc.scalar.activation(h_hi[:, k], x[:, k], ACT.Copy, scale=par[:, k:k + 1]).then_inc(h_hi_ready, 1)
                if k == 0:
                    first_block_hi(1)
                    first_block_hi(2)
                if k >= 2:
                    act.wait_ge(summed, max(k - 2, 1) + 1)
                nc.scalar.activation(T[2 + k % 2][:], x[:, k], ACT.Square).then_inc(square_ready, 1)
            with act.Fori(0, DEPTH) as l:
                ffn(l, 0)
                act.wait_ge(params_loaded, (l + 2) * 16)
                before(l, 0, PRE[1])
                for e in range(len(MIX_STEPS)):
                    mix_step(l, e)
                for k in range(OUT_AT, MIX_BLOCKS):
                    split_hi(l, MIX_AT + k + AHEAD)
                    if k == OUT_AT + 1:
                        after_half(l, 1, 0)
                after_half(l, 1, 1)
                before(l, 1, PRE[2])
                ffn(l, 1)
                before(l, 2, NEXT_PRE)

        @block.vector
        def _(vec):
            links = [0]

            def link(l, ins):
                links[0] += 1
                ins.then_inc(chain, 1)
                vec.wait_ge(chain, l * VECTOR_LINKS + links[0])

            def split_lo(l, k):
                slot = k % RING
                vec.wait_ge(block_hi, n_block(l, k + 1))
                nc.vector.tensor_tensor(w_lo[:, slot], raw[:, slot], w_hi[:, slot], ALU.subtract)\
                    .then_inc(block_split, 1)

            def h_low(n, k, gain):
                vec.wait_ge(h_hi_ready, n)
                nc.vector.scalar_tensor_tensor(h_lo[:, k], x[:, k], par[:, gain + k:gain + k + 1],
                                               h_hi[:, k], ALU.mult, ALU.subtract).then_inc(h_ready, 1)

            def inverse_root(l, dst):
                guess = dst.bitcast(I32)
                link(l, nc.vector.tensor_scalar(guess, mean_sq[:].bitcast(I32), 1, None,
                                                ALU.logical_shift_right))
                link(l, nc.vector.tensor_scalar(guess, guess, -1, 0x5F1FFFF9, ALU.mult, ALU.add))
                link(l, nc.vector.tensor_tensor(newton[:], dst, dst, ALU.mult))
                link(l, nc.vector.scalar_tensor_tensor(newton[:], newton[:], -0.703952253 * 0.375, mean_sq[:],
                                                       ALU.mult, ALU.mult))
                link(l, nc.vector.scalar_tensor_tensor(dst, newton[:], 2.38924456 * 0.703952253 * 0.375, dst,
                                                       ALU.add, ALU.mult))
                link(l, nc.vector.tensor_tensor(newton[:], dst, dst, ALU.mult))
                link(l, nc.vector.scalar_tensor_tensor(newton[:], newton[:], 64.0 / 9.0, mean_sq[:],
                                                       ALU.mult, ALU.mult))
                link(l, nc.vector.scalar_tensor_tensor(newton[:], newton[:], -10.0 / 3.0, newton[:],
                                                       ALU.add, ALU.mult))
                link(l, nc.vector.scalar_tensor_tensor(dst, newton[:], 5.0, dst, ALU.add, ALU.mult))

            def scale_columns(l, s, post):
                src = bank[1 if post else 4]
                vec.wait_ge(cols_ready, n_columns(l, s, post) + 1)
                link(l, nc.vector.tensor_scalar(mean_sq[:], src[:, 0:NT], 1.0 / D_MODEL, RMS_EPS,
                                                ALU.mult, ALU.add))
                inverse_root(l, rcol[:])
                nc.vector.tensor_tensor(
                    T[0][:].rearrange("p (t j) -> p t j", t=NT),
                    ident[:].unsqueeze(1).broadcast_to([P, NT, P]),
                    rcol[:].unsqueeze(2).broadcast_to([P, NT, P]), ALU.mult).then_inc(diag_ready, 1)

            def scale_tile(l, s, post):
                vec.wait_ge(scale_ready, n_norm(l, s, post) + 1)
                link(l, nc.vector.tensor_copy(scale_b[:], bank[3 if post else 5][:]))

            def update(l, s):
                scale_columns(l, s, 1)
                vec.wait_ge(scale_ready, n_norm(l, s, 1) + 1)
                gain = (PRE[1], PRE[2], NEXT_PRE)[s]
                for k in range(KT):
                    if k == 1:
                        vec.wait_ge(scale_twin, l * 3 + (s + 1))
                    if k == 4:
                        vec.wait_ge(scale_copied, l * 3 + (s + 2))
                    src, scale = (y[:, k], bank[3][:]) if k < 4 else (bank[k][:], scale_b[:])
                    g = PRE[s] + 8 + k
                    nc.vector.scalar_tensor_tensor(T[(k + 1) % 2][:], src, par[:, g:g + 1], scale,
                                                   ALU.mult, ALU.mult).then_inc(y_scaled, 1)
                    if k:
                        h_low(n_tile(l, s + 1, k), k - 1, gain)
                    vec.wait_ge(y_scaled, n_tile(l, s, k + 1))
                    nc.vector.tensor_tensor(x[:, k], x[:, k], T[(k + 1) % 2][:], ALU.add).then_inc(x_ready, 1)
                h_low(n_tile(l, s + 1, KT), KT - 1, gain)

            def gate(l, part, n, f, used_at):
                vec.wait_ge(block_used, used_at)
                nc.vector.tensor_tensor(T[0][:], bank[2 * (f % 2)][:], scale_b[:], ALU.mult)\
                    .then_inc(bank_scaled, 1)

            def hidden(l, part, n, f, f_at, used_at):
                vec.wait_ge(block_used, used_at)
                nc.vector.tensor_tensor(T[2][:], bank[2 * (f % 2) + 1][:], scale_b[:], ALU.mult)\
                    .then_inc(bank_scaled, 1)
                vec.wait_ge(silu_ready, n + 1)
                vec.wait_ge(bank_scaled, n * 2 + 2)
                nc.vector.tensor_tensor(T[3][:], T[1][:], T[2][:], ALU.mult).then_inc(hidden_ready, 1)
                vec.wait_ge(hidden_hi, n + 1)
                nc.vector.tensor_tensor(a_lo[:, f_at], T[3][:], a_hi[:, f_at], ALU.subtract)\
                    .then_inc(hidden_split, 1)

            def ffn(l, part):
                k0 = FFN_AT[part]
                s = 2 * part
                split_lo(l, k0 + 3)
                scale_columns(l, s, 0)
                split_lo(l, k0 + 4)
                scale_tile(l, s, 0)
                at = lambda b: n_block(l, k0 + b + 1) + RING
                gate(l, part, n_hidden(l, part, 0), 0, at(0))
                hidden(l, part, n_hidden(l, part, 0), 0, 0, at(1))
                split_lo(l, k0 + 5)
                gate(l, part, n_hidden(l, part, 1), 1, at(2))
                split_lo(l, k0 + 6)
                hidden(l, part, n_hidden(l, part, 1), 1, 1, at(3))
                with vec.Fori(0, UP_BLOCKS // RING - 1) as i:
                    for f in (2, 3):
                        n = l * (2 * FT) + i * 2 + (FT * part + f)
                        for b in (0, 1):
                            j = k0 + 2 * f + b + AHEAD
                            vec.wait_ge(block_hi, l * LAYER_BLOCKS + i * RING + (j + 1))
                            nc.vector.tensor_tensor(w_lo[:, j % RING], raw[:, j % RING], w_hi[:, j % RING],
                                                    ALU.subtract).then_inc(block_split, 1)
                            done = l * LAYER_BLOCKS + i * RING + (k0 + 2 * f + b + 1 + RING)
                            if b == 0:
                                gate(l, part, n, f, done)
                            else:
                                hidden(l, part, n, f, i * 2 + f, done)
                if part == 0:
                    vec.wait_ge(params_loaded, (l + 2) * 16)
                    for g in (PRE[0] + 8, PRE[2] + 8):
                        link(l, nc.vector.tensor_scalar(par[:, g:g + 8], par[:, g:g + 8], 0.5, None, ALU.mult))
                for half in (0, 1):
                    k1 = k0 + UP_BLOCKS + half * DOWN_BLOCKS
                    split_lo(l, k1 + AHEAD)
                    with vec.Fori(0, 2) as i:
                        for b in range(RING):
                            j = k1 + 1 + b + AHEAD
                            vec.wait_ge(block_hi, l * LAYER_BLOCKS + i * RING + (j + 1))
                            nc.vector.tensor_tensor(w_lo[:, j % RING], raw[:, j % RING], w_hi[:, j % RING],
                                                    ALU.subtract).then_inc(block_split, 1)
                    for b in (9, 10):
                        split_lo(l, k1 + b + AHEAD)
                update(l, s)

            def mlp_argument(l, m):
                vec.wait_ge(mlp_done, l * 3 + (m + 1))
                link(l, nc.vector.tensor_scalar(T[0][:], bank[m][:], par[:, FILT_B + m:FILT_B + m + 1],
                                                par[:, FILT_B + 3:FILT_B + 4], ALU.add, ALU.mult))
                link(l, nc.vector.tensor_scalar(T[1][:], T[0][:], 1.0 / TWO_PI, ROUND, ALU.mult, ALU.add))
                link(l, nc.vector.tensor_scalar(T[1][:], T[1][:], ROUND, -TWO_PI, ALU.subtract, ALU.mult))
                link(l, nc.vector.tensor_tensor(T[0][:], T[0][:], T[1][:], ALU.add))
                nc.vector.tensor_scalar(T[0][:], T[0][:], PI_BELOW, -PI_BELOW, ALU.min, ALU.max)\
                    .then_inc(mlp_arg, 1)
                if m == 2:
                    vec.wait_ge(mlp_sin, l * 3 + 3)
                    nc.vector.memset(hid[HEAD_DIM:P, 0:1], 0.0).then_inc(hid_ready, 1)

            def mix_step(l, e):
                kind, n, blks, _, first = MIX_STEPS[e]
                late = kind in ("u", "g1", "g2", "kernel_cos", "kernel_sin", "forward_low", "forward_high")\
                    or (kind == "z" and n == 3)

                def split_block():
                    split_lo(l, MIX_AT + blks[0] + AHEAD)

                if not late:
                    for k in blks[:1] if kind == "inverse" else blks:
                        split_lo(l, MIX_AT + k + AHEAD)
                        if kind == "v" and k in MLP_IN_V:
                            mlp_argument(l, MLP_IN_V[k])
                if kind == "z" and n == 0:
                    return
                if kind == "z" and n == 1:
                    scale_columns(l, 1, 0)
                    return
                if kind == "z" and n == 2:
                    scale_tile(l, 1, 0)
                    for m in (0, 1, 2):
                        scale_projection(l, e - 2 + m, "z", m, bank[m])
                    for m in (0, 1, 2):
                        convolve(l, e - 2 + m, "z", m)
                elif kind in ("z", "g1", "g2"):
                    scale_projection(l, e, kind, n, bank[first + n])
                    if kind == "z":
                        mlp_argument(l, 0)
                    split_block()
                    convolve(l, e, kind, n)
                elif kind == "v":
                    for t in range(NT):
                        vec.wait_ge(staged, n_staged(l, e, t + 1))
                        nc.vector.bn_stats(stats[:, t], v[:, t]).then_inc(result_read, 1)
                    vec.wait_ge(result_read, n_read(l, e, 4))
                    vec.sem_inc(stats_go, 1)
                    for t in range(NT):
                        ins = nc.vector.bn_aggr(mv[:, t], stats[:, t])
                    link(l, ins)
                    link(l, nc.vector.tensor_scalar(mean_sq[:], mv[:, :, 1], LN_EPS, None, ALU.add))
                    inverse_root(l, rstd[:])
                    for t in range(NT):
                        nc.vector.tensor_scalar(v[:, t], v[:, t], mv[:, t, 0:1], rstd[:, t:t + 1],
                                                ALU.subtract, ALU.mult).then_inc(ln_centred, 1)
                elif kind == "u":
                    wait_result(vec, l, e, 1)
                    nc.vector.tensor_tensor(T[n % 2][:], bank[first + n][:], scale_b[:], ALU.mult)\
                        .then_inc(result_read, 1)
                    split_block()
                    vec.wait_ge(staged, n_staged(l, e, 1))
                elif kind in ("filter_sum", "filter_diff"):
                    diff = kind == "filter_diff"
                    vec.wait_ge(decay_loaded, (l + 1) * 16)
                    if not diff:
                        wait_result(vec, l, e, 4)
                        nc.vector.tensor_scalar(wo[HEAD_DIM:P, :], wo[HEAD_DIM:P, :], -1.0, None, ALU.mult)\
                            .then_inc(negated, 1)
                    for j in range(4):
                        if diff:
                            wait_result(vec, l, e, j + 1)
                        nc.vector.tensor_tensor(to_split[:, j + 4 * diff], bank[first + j][:], decay_sb[:, j],
                                                ALU.mult).then_inc(result_read, 1)
                    if not diff:
                        filter_low(l, e, 0)
                elif kind == "diff_low":
                    filter_low(l, STEP_AT[("filter_diff", n)], 4)
                elif kind == "fold_parts":
                    src = g1 if n else zg2
                    for c in range(4):
                        late_half, early_half = src[:, c, HALF_SEQ:SEQ], src[:, c, HALF_SEQ - 1::-1]
                        nc.vector.tensor_tensor(fold_src[:, c, 0:HALF_SEQ], late_half, early_half, ALU.add)
                        nc.vector.tensor_tensor(fold_src[:, c, HALF_SEQ:SEQ], late_half, early_half,
                                                ALU.subtract).then_inc(fold_ready, 1)
                elif kind == "fold":
                    if n == 0:
                        vec.wait_ge(gmlp_ready, l * 4 + 4)
                    for q in range(4):
                        vec.wait_ge(staged, n_staged(l, e, q + 1))
                        nc.vector.tensor_tensor(fold_lo[:, q], bank[first + q][:], fold_hi[:, q],
                                                ALU.subtract).then_inc(result_read, 1)
                elif kind == "gmlp":
                    wait_result(vec, l, e, 4)
                    for c in range(4):
                        bias = pk[:, PK_BS + c * P:PK_BS + (c + 1) * P].unsqueeze(1).broadcast_to([P, NT, P])
                        nc.vector.tensor_tensor(v[:, c].rearrange("p (t j) -> p t j", t=NT),
                                                bank[first + c][:].rearrange("p (t j) -> p t j", t=NT),
                                                bias, ALU.add).then_inc(result_read, 1)
                elif kind == "gmlp_gate":
                    for c in range(4):
                        vec.wait_ge(result_read, n_read(l, STEP_AT[("gmlp", 0)], c + 1))
                        nc.vector.tensor_tensor(u[:, c], v[:, c], u[:, c], ALU.mult).then_inc(gmlp_ready, 1)
                elif kind in ("kernel_cos", "kernel_sin"):
                    o = 4 * (kind == "kernel_sin")
                    for i in (0, 1):
                        vec.wait_ge(staged, n_staged(l, e, i + 1))
                        even, odd = k_spec[:, o + i], bank[first + 2 + i][:]
                        if o:
                            ins = nc.vector.scalar_tensor_tensor(k_spec[:, o + 2 + i], even, -1.0, odd,
                                                                 ALU.mult, ALU.add)
                        else:
                            ins = nc.vector.tensor_tensor(k_spec[:, o + 2 + i], even, odd, ALU.subtract)
                        ins.then_inc(result_read, 1)
                    for i in (0, 1):
                        vec.wait_ge(result_read, n_read(l, e, i + 1))
                        nc.vector.tensor_tensor(k_spec[:, o + i], k_spec[:, o + i], bank[first + 2 + i][:],
                                                ALU.add).then_inc(result_read, 1)
                    split_block()
                    vec.wait_ge(result_read, n_read(l, e, 4))
                elif kind in ("forward_low", "forward_high"):
                    wait_result(vec, l, e, 4)
                    for i in (0, 1):
                        q = i + 2 * (kind == "forward_high")
                        re, im = bank[first + i][:], bank[first + 2 + i][:]
                        k_re, k_im = k_spec[:, q], k_spec[:, 4 + q]
                        nc.vector.tensor_tensor(to_split[:, q], re, k_re, ALU.mult)
                        nc.vector.tensor_tensor(T[2 * i][:], im, k_im, ALU.mult).then_inc(result_read, 1)
                        nc.vector.tensor_tensor(to_split[:, 4 + q], re, k_im, ALU.mult)
                        nc.vector.tensor_tensor(T[2 * i + 1][:], im, k_re, ALU.mult).then_inc(result_read, 1)
                    split_block()
                    for i in (0, 1):
                        q = i + 2 * (kind == "forward_high")
                        for part in (0, 1):
                            vec.wait_ge(staged, n_staged(l, e, 2 * i + part + 1))
                            nc.vector.tensor_tensor(s_lo[:, 4 * part + q], to_split[:, 4 * part + q],
                                                    s_hi[:, 4 * part + q], ALU.subtract)\
                                .then_inc(spectrum_split, 1)
                elif kind == "inverse":
                    for c in range(4):
                        vec.wait_ge(staged, n_staged(l, e, c + 1))
                        even, odd = T[2 + c % 2][:, 0:HALF_SEQ], bank[first + c][:, HALF_SEQ:SEQ]
                        nc.vector.tensor_tensor(T[c % 2][:, HALF_SEQ:SEQ], even, odd, ALU.subtract)
                        nc.vector.tensor_tensor(T[c % 2][:, HALF_SEQ - 1::-1], even, odd, ALU.add)\
                            .then_inc(result_read, 1)
                        vec.wait_ge(result_read, n_read(l, e, c + 1))
                        if n == 0:
                            link(l, nc.vector.tensor_tensor(g1[:, c], g1[:, c], T[c % 2][:], ALU.mult))
                        else:
                            nc.vector.tensor_tensor(zg2[:, c], zg2[:, c], T[c % 2][:], ALU.mult)\
                                .then_inc(gated, 1)
                            if c % 2:
                                cat_yb(l, c - 1)
                                cat_yb(l, c)
                    split_lo(l, MIX_AT + blks[1] + AHEAD)

            def filter_low(l, e, at):
                for j in range(4):
                    vec.wait_ge(staged, n_staged(l, e, j + 1))
                    nc.vector.tensor_tensor(s_lo[:, at + j], to_split[:, at + j], s_hi[:, at + j], ALU.subtract)\
                        .then_inc(filter_split, 1)

            def cat_yb(l, c):
                vec.wait_ge(cat_hi, l * 8 + (4 + c + 1))
                nc.vector.tensor_tensor(h_lo[:, 4 + c], zg2[:, c], h_hi[:, 4 + c], ALU.subtract)\
                    .then_inc(cat_split, 1)

            def scale_projection(l, e, kind, n, src):
                wait_result(vec, l, e, 1)
                nc.vector.tensor_tensor(scaled(kind, n)[:], src[:], scale_b[:], ALU.mult).then_inc(result_read, 1)

            def convolve(l, e, kind, n):
                c = n + {"z": 0, "g1": 4, "g2": 8}[kind]
                dst = {"z": zg2, "g1": g1, "g2": zg2}[kind]
                src = scaled(kind, n)
                vec.wait_ge(staged, n_staged(l, e, 1))
                link(l, nc.vector.scalar_tensor_tensor(
                    dst[:, n, 1:SEQ], src[:, 0:SEQ - 1], par[:, CONV_W + c:CONV_W + c + 1],
                    dst[:, n, 1:SEQ], ALU.mult, ALU.add))
                link(l, nc.vector.scalar_tensor_tensor(
                    dst[:, n, 0:SEQ - 1], src[:, 1:SEQ], par[:, CONV_W + 24 + c:CONV_W + 25 + c],
                    dst[:, n, 0:SEQ - 1], ALU.mult, ALU.add))

            nc.vector.sem_inc(block_split, RING)
            nc.vector.sem_inc(x_ready, 1)
            for k in range(KT):
                for j in {0: (0,), 1: (1, 2)}.get(k, ()):
                    vec.wait_ge(block_hi, j + 1)
                    nc.vector.tensor_tensor(w_lo[:, j], raw[:, j], w_hi[:, j], ALU.subtract)\
                        .then_inc(block_split, 1)
                h_low(k + 1, k, 0)
            vec.wait_ge(tables_loaded, 16)
            with vec.Fori(0, DEPTH) as l:
                ffn(l, 0)
                for e in range(len(MIX_STEPS)):
                    mix_step(l, e)
                for k in range(OUT_AT, MIX_BLOCKS):
                    split_lo(l, MIX_AT + k + AHEAD)
                update(l, 1)
                ffn(l, 1)
            assert links[0] == VECTOR_LINKS, links

        @block.tensor
        def _(pe):
            def three(dst, w, m, start, stop):
                nc.tensor.matmul(dst, w[0], m[0], start=start, stop=False)
                nc.tensor.matmul(dst, w[0], m[1], start=False, stop=False)
                return nc.tensor.matmul(dst, w[1], m[0], start=False, stop=stop)

            def w_part(slot, a, b):
                return w_hi[:, slot, a:b], w_lo[:, slot, a:b]

            def h_part(k, a=0, b=SEQ):
                return h_hi[:, k, a:b], h_lo[:, k, a:b]

            def have_block(l, k):
                pe.wait_ge(block_split, n_block(l, k + 1) + RING)

            def first_tiles(l, s, k, dsts):
                for j in range(3):
                    have_block(l, k + j)
                for t in range(KT):
                    pe.wait_ge(h_ready, n_tile(l, s, t + 1))
                    for j, dst in enumerate(dsts):
                        if t == 0 and j == 2:
                            pe.wait_ge(scale_copied, l * 3 + (s + 1))
                        ins = three(dst, w_part((k + j) % RING, t * P, (t + 1) * P), h_part(t), t == 0, t == KT - 1)
                        if t == KT - 1:
                            used(ins)

            def column_tile(l, k, dst, spread_of=None):
                have_block(l, k)
                slot = k % RING
                for t in range(KT):
                    ins = three(dst, w_part(slot, t * P, (t + 1) * P), h_part(t), t == 0, t == KT - 1)
                    if t == 4 and spread_of is not None:
                        spread(l, spread_of, 0)
                return ins

            def columns(l, s, post):
                dst = bank[1 if post else 4]
                sources = (hid, T[2], T[3]) if post else (hid,)
                for i, src in enumerate(sources):
                    if i == 0:
                        pe.wait_ge(summed, n_summed(l, s, post, 5 if post else 7))
                    else:
                        pe.wait_ge(square_ready, n_square(l, s, post, 6 + i))
                    for t in range(NT):
                        ins = nc.tensor.matmul(dst[:, 0:NT], src[:, t * P:(t + 1) * P], unit[:, t],
                                               start=i == 0 and t == 0, stop=src is sources[-1] and t == NT - 1)
                ins.then_inc(cols_ready, 1)

            def spread(l, s, post):
                pe.wait_ge(diag_ready, n_norm(l, s, post) + 1)
                nc.tensor.matmul(bank[3 if post else 5][:], ones[:], T[0][:], start=True, stop=True)\
                    .then_inc(scale_ready, 1)
                if post:
                    nc.tensor.matmul(bank[2][:], ones[:], T[0][:], start=True, stop=True)\
                        .then_inc(scale_twin, 1)

            def keep_clock(count):
                for _ in range(count):
                    nc.tensor.matmul(bank[0][:, 0:P], ident[:], ident[:], start=True, stop=True)

            def used(ins):
                ins.then_inc(block_used, 1)

            def ffn(l, part):
                k0 = FFN_AT[part]
                s = 2 * part
                first_tiles(l, s, k0, [bank[b][:] for b in range(3)])
                columns(l, s, 0)
                used(column_tile(l, k0 + 3, bank[3][:], s))
                with pe.Fori(0, UP_BLOCKS // RING - 1) as i:
                    for b in range(RING):
                        f, up = b // 2, b % 2
                        pe.wait_ge(bank_scaled, l * (4 * FT) + i * 4 + (2 * FT * part + b + 1))
                        pe.wait_ge(block_split, l * LAYER_BLOCKS + i * RING + (k0 + RING + b + 1 + RING))
                        slot = (k0 + b) % RING
                        dst = bank[2 * f + up][:]
                        for t in range(KT):
                            ins = three(dst, w_part(slot, t * P, (t + 1) * P), h_part(t), t == 0, t == KT - 1)
                        used(ins)
                for half in (0, 1):
                    k1 = k0 + UP_BLOCKS + half * DOWN_BLOCKS
                    down_block(l, s, k1, 0, half, True, False, hidden_pair, n_hidden(l, part, 2))
                    with pe.Fori(0, 2) as i:
                        for b in range(RING):
                            j = k1 + 1 + b
                            pe.wait_ge(block_split, l * LAYER_BLOCKS + i * RING + (j + 1 + RING))
                            if half == 0:
                                pe.wait_ge(hidden_split, l * (2 * FT) + i * (2 * RING) + (FT * part + 2 * b + 4))
                            for d in range(4):
                                for t in range(2):
                                    f_at = i * (2 * RING) + (2 * b + 2 + t)
                                    ins = three(bank[4 + d][:],
                                                w_part(j % RING, t * 512 + d * P, t * 512 + (d + 1) * P),
                                                (a_hi[:, f_at], a_lo[:, f_at]), False, False)
                            used(ins)
                    down_block(l, s, k1 + 9, 9, half, False, False, hidden_pair, n_hidden(l, part, 20))
                    down_block(l, s, k1 + 10, 10, half, False, True, hidden_pair, n_hidden(l, part, 22))
                columns(l, s, 1)
                keep_clock(12)
                spread(l, s, 1)
                keep_clock(8)

            def hidden_pair(f):
                return a_hi[:, f], a_lo[:, f]

            def down_block(l, s, k, j, half, first, last, pair, split_count):
                have_block(l, k)
                if split_count is not None and half == 0:
                    pe.wait_ge(hidden_split, split_count)
                slot = k % RING
                for d in range(4):
                    if first and half == 1:
                        pe.wait_ge(square_ready, n_square(l, s, 1, d + 1))
                    for t in range(2):
                        ins = three(bank[4 + d][:], w_part(slot, t * 512 + d * P, t * 512 + (d + 1) * P),
                                    pair(2 * j + t), first and t == 0, last and t == 1)
                    if last and d < 3:
                        ins.then_inc(y_done, 1)
                used(ins)

            def mix_step(l, e):
                kind, n, blks, m, first = MIX_STEPS[e]
                slots = [(MIX_AT + k) % RING for k in blks]

                def free(b):
                    prev = last_in_bank(e, b)
                    if prev is not None:
                        pe.wait_ge(result_read, l * RESULTS + (prev + 1))

                if kind in ("z", "u", "g1", "g2"):
                    if kind == "z" and n < 3:
                        if n == 0:
                            first_tiles(l, 1, MIX_AT, [bank[b][:] for b in range(3)])
                            columns(l, 1, 0)
                        return
                    free(first + n)
                    used(column_tile(l, MIX_AT + blks[0], bank[first + n][:], 1 if kind == "z" else None))
                elif kind == "v":
                    for j, k in enumerate(blks):
                        have_block(l, MIX_AT + k)
                        if j == 0:
                            pe.wait_ge(result_read, l * RESULTS + 1)
                        for t in range(NT):
                            for kk in range(2):
                                hp = h_part(2 * j + kk, t * P, (t + 1) * P)
                                ins = three(bank[4 + t][:], hp, w_part(slots[j], kk * 512, (kk + 1) * 512),
                                            j == 0 and kk == 0, j == 3 and kk == 1)
                            if j == 3 and t < 3:
                                ins.then_inc(result, 1)
                        used(ins)
                        if k in MLP_IN_V:
                            mlp_layer(l, MLP_IN_V[k])
                elif kind == "mlp":
                    free(n)
                    mlp_layer(l, n)
                elif kind in ("filter_sum", "filter_diff"):
                    pe.wait_ge(filt_loaded, l * 32 + 16 * (n + 1))
                    pe.wait_ge(hid_ready, l + 1)
                    if kind == "filter_diff":
                        pe.wait_ge(negated, l * 2 + (n + 1))
                    elif n:
                        pe.wait_ge(skip_loaded, (l + 1) * 16)
                    for j in range(4):
                        free(first + j)
                        with_skip = j == 0 and kind == "filter_sum"
                        ins = nc.tensor.matmul(bank[first + j][:], hid[:, j * P:(j + 1) * P], wo[:],
                                               start=True, stop=not with_skip)
                        if with_skip:
                            skip = skip_row[0:1, :] if n else pk[0:1, PK_SKIP:PK_SKIP + D_B]
                            ins = nc.tensor.matmul(bank[first][:], ident[0:1, :], skip, start=False, stop=True)
                        ins.then_inc(result, 1)
                elif kind == "fold":
                    pe.wait_ge(fold_ready, l * 8 + (4 * n + 4))
                    for q in range(4):
                        free(first + q)
                        for c in range(4):
                            ins = nc.tensor.transpose(bank[first + q][:, c * P:(c + 1) * P],
                                                      fold_src[:, c, q * P:(q + 1) * P], ident[:])
                    ins.then_inc(fold_turned, 1)
                elif kind == "gmlp":
                    for c in range(4):
                        free(first + c)
                        for t in range(NT):
                            if c == 0:
                                pe.wait_ge(ln_ready, l * NT + (t + 1))
                            for side in (0, 1):
                                hd = 2 * c + side
                                ins = nc.tensor.matmul(
                                    bank[first + c][64 * side:64 * side + 64, t * P:(t + 1) * P],
                                    v[:, t, hd * HEAD_DIM:(hd + 1) * HEAD_DIM],
                                    pk[:, PK_WS + hd * P:PK_WS + (hd + 1) * P], start=True, stop=True)
                        ins.then_inc(result, 1)
                elif kind in ("kernel_cos", "kernel_sin"):
                    sin = kind == "kernel_sin"
                    have_block(l, MIX_AT + blks[0])
                    pe.wait_ge(filter_split, l * 16 + (8 * n + 4 + 4 * sin))
                    for parity in (0, 1):
                        for i in (0, 1):
                            free(first + 2 * parity + i)
                            for t in (0, 1):
                                j = 2 * parity + t
                                ins = three(bank[first + 2 * parity + i][:],
                                            w_part(slots[0], j * 256 + i * P, j * 256 + (i + 1) * P),
                                            (s_hi[:, 4 * sin + j], s_lo[:, 4 * sin + j]), t == 0, t == 1)
                    used(ins)
                elif kind in ("forward_low", "forward_high"):
                    have_block(l, MIX_AT + blks[0])
                    for s in (0, 1):
                        for i in (0, 1):
                            free(first + 2 * s + i)
                            for t in (0, 1):
                                a = t * 512 + s * 256 + i * P
                                ins = three(bank[first + 2 * s + i][:], w_part(slots[0], a, a + P),
                                            (fold_hi[:, 2 * s + t], fold_lo[:, 2 * s + t]), t == 0, t == 1)
                    used(ins)
                elif kind == "inverse":
                    for side, k in enumerate(blks):
                        have_block(l, MIX_AT + k)
                        for i in range(16):
                            q, c = (i // 4, i % 4) if side == 0 else (i % 4, i // 4)
                            if side == 0 and c == 0:
                                pe.wait_ge(spectrum_split, l * 16 + (8 * n + 2 * q + 1))
                            elif side == 1 and i == 0:
                                pe.wait_ge(spectrum_split, l * 16 + (8 * n + 8))
                            if side == 0 and q == 0:
                                free(first + c)
                            j = 4 * side + q
                            ins = three(bank[first + c][:, side * HALF_SEQ:(side + 1) * HALF_SEQ],
                                        (s_hi[:, j, c * P:(c + 1) * P], s_lo[:, j, c * P:(c + 1) * P]),
                                        w_part(slots[side], q * 256, (q + 1) * 256), q == 0, q == 3)
                            if side == 1 and q == 3 and c < 3:
                                ins.then_inc(result, 1)
                        used(ins)
                elif kind == "out_a":
                    if n == 0:
                        for b in range(4, 8):
                            free(b)
                        pe.wait_ge(cat_split, l * 8 + 4)
                    down_block(l, 1, MIX_AT + blks[0], n, 0, n == 0, False, h_part, None)

            def mlp_layer(l, m):
                if m == 0:
                    pe.wait_ge(pack_loaded, (l + 1) * 16)
                    rhs = pk[0:64, PK_Z:PK_Z + SEQ]
                else:
                    pe.wait_ge(mlp_sin, l * 3 + m)
                    rhs = T[2][0:64, :]
                    pe.wait_ge(result_read, l * RESULTS + 3)
                nc.tensor.matmul(bank[m][:], pk[0:64, PK_W + P * m:PK_W + P * (m + 1)], rhs,
                                 start=True, stop=True).then_inc(mlp_done, 1)

            pe.sem_inc(block_used, RING)
            pe.sem_inc(cols_ready, 1)
            pe.sem_inc(scale_copied, 1)
            pe.wait_ge(tables_loaded, 16)
            pe.wait_ge(ones_ready, 2 + NT)
            keep_clock(12)
            with pe.Fori(0, DEPTH) as l:
                ffn(l, 0)
                for e in range(len(MIX_STEPS)):
                    mix_step(l, e)
                for j in (2, 3):
                    pe.wait_ge(cat_split, l * 8 + 2 * (j + 1))
                    down_block(l, 1, MIX_AT + OUT_AT - 2 + j, j, 0, False, j == 3, h_part, None)
                for j in range(4):
                    down_block(l, 1, MIX_AT + OUT_AT + 2 + j, j, 1, j == 0, j == 3, h_part, None)
                columns(l, 1, 1)
                keep_clock(12)
                spread(l, 1, 1)
                keep_clock(8)
                ffn(l, 1)



def transform_tables():
    f_low = np.arange(256)
    freq = np.concatenate([f_low, 511 - f_low])
    lag = np.concatenate([np.arange(0, SEQ, 2), np.arange(1, SEQ, 2)])
    kern = np.pi * np.outer(lag, 2 * f_low + 1) / 1024
    time = np.pi * np.outer(np.arange(256) + 0.5, 2 * freq + 1) / 1024
    blk = lambda a, n: a.astype(np.float32).reshape(n, P, BLOCK // n).transpose(1, 0, 2).reshape(P, BLOCK)
    kernel_cos, kernel_sin = blk(np.cos(kern), 4), blk(-np.sin(kern), 4)
    low = blk(np.concatenate([np.cos(time[:, :256]), -np.sin(time[:, :256])], 1), 2)
    high = blk(np.concatenate([np.cos(time[:, 256:]), -np.sin(time[:, 256:])], 1), 2)
    inv_cos, inv_sin = blk(np.cos(time).T / 512, 4), blk(np.sin(time).T / 512, 4)
    return kernel_cos, kernel_sin, low, high, inv_cos, inv_sin, lag


def filter_tables(lag):
    f32 = np.float32
    t = np.linspace(0.0, 1.0, SEQ, dtype=f32)
    bands = np.linspace(1e-4, 15, 16, dtype=f32)
    ang = f32(2.0 * np.pi / SEQ) * np.arange(SEQ, dtype=f32)[:, None] * bands[None, :]
    z = np.zeros((64, SEQ), f32)
    z[:FILTER_EMB] = np.concatenate([t[:, None], np.cos(ang), -np.sin(ang)], -1)[lag].T
    low, high = np.log(1e-2) / 1.5, np.log(1e-2) / 0.3
    deltas = np.abs(np.linspace(low, high, D_B, dtype=f32))
    decay = np.exp(-t[lag][:, None] * deltas).astype(f32)
    return z, decay.reshape(4, P, D_B).transpose(1, 0, 2)



def kernel(**inputs):
    import concourse.bacc as _bacc
    from concourse.bass_utils import run_bass_kernel_spmd as _run

    a = {k: np.asarray(w) for k, w in inputs.items()}
    L = DEPTH
    kc, ks, fl, fh, ic, is_, lag = transform_tables()
    z, decay = filter_tables(lag)

    def column_blocks(w):
        n = w.shape[1] // P
        return w.reshape(KT, P, n, P).transpose(2, 1, 0, 3).reshape(n, P, BLOCK)

    def row_blocks(w):
        n = w.shape[0] // (2 * P)
        return w.reshape(n, 2, P, 512).transpose(0, 2, 1, 3).reshape(n, P, BLOCK)

    stream = np.zeros((L * LAYER_BLOCKS + PADDING, P, BLOCK), np.float32)
    blocks = stream[:L * LAYER_BLOCKS].reshape(L, LAYER_BLOCKS, P, BLOCK)
    for l in range(L):
        for part in (0, 1):
            k0 = part * (FFN_BLOCKS + MIX_BLOCKS)
            name = f"ffn{part + 1}_w_"
            blocks[l, k0:k0 + UP_BLOCKS:2] = column_blocks(a[name + "gate"][l])
            blocks[l, k0 + 1:k0 + UP_BLOCKS:2] = column_blocks(a[name + "up"][l])
            for half in (0, 1):
                k1 = k0 + UP_BLOCKS + half * DOWN_BLOCKS
                blocks[l, k1:k1 + DOWN_BLOCKS] = row_blocks(a[name + "down"][l][:, half * 512:half * 512 + 512])
        w, mix = a["mix_w_in"][l], blocks[l, FFN_BLOCKS:FFN_BLOCKS + MIX_BLOCKS]
        out_w = a["mix_w_out"][l]
        out_first, out_second = row_blocks(out_w[:, 0:512]), row_blocks(out_w[:, 512:1024])
        by_step = {"z": column_blocks(w[:, 1024:1536]), "u": column_blocks(w[:, 0:512]),
                   "g1": column_blocks(w[:, 1536:2048]), "g2": column_blocks(w[:, 2048:2560]),
                   "v": [row_blocks(w[:, 512:1024])], "out_a": out_first, "inverse": [(ic, is_)] * 2,
                   "kernel_cos": (kc, kc), "kernel_sin": (ks, ks), "forward_low": (fl, fl),
                   "forward_high": (fh, fh)}
        for kind, n, blks, _, _ in MIX_STEPS:
            if blks:
                mix[blks[0]:blks[-1] + 1] = by_step[kind][n]
        mix[OUT_AT:OUT_AT + 2], mix[OUT_AT + 2:] = out_first[2:4], out_second

    params = np.empty((L, PARAMS, P), np.float32)
    for l in range(L):
        for i, name in enumerate(("ffn1_pre_g", "ffn1_post_g", "mix_pre_g", "mix_post_g",
                                  "ffn2_pre_g", "ffn2_post_g")):
            params[l, 8 * i:8 * i + 8] = a[name][l].reshape(KT, P)
        params[l, CONV_W:CONV_W + 36] = a["hy_conv_w"][l].reshape(36, P)
        params[l, CONV_B:CONV_B + 12] = a["hy_conv_b"][l].reshape(12, P)
        for i, name in enumerate(("b1", "b2", "b3", "freq")):
            params[l, FILT_B + i] = np.tile(a["hy_filt_" + name][l], 2)
        params[l, NEXT_PRE:NEXT_PRE + 8] = a["ffn1_pre_g"][min(l + 1, L - 1)].reshape(KT, P)

    pack = np.zeros((L, P, PACK), np.float32)
    filt_out = np.empty((L, 2, P, D_B), np.float32)
    for l in range(L):
        pack[l, :, PK_WS:PK_WS + 1024] = a["gmlp_w_s"][l].transpose(2, 0, 1).reshape(P, HEADS * P)
        pack[l, :, PK_LNG:PK_LNG + 512] = a["gmlp_ln_g"][l]
        pack[l, :, PK_LNB:PK_LNB + 512] = a["gmlp_ln_b"][l]
        bias = a["gmlp_b_s"][l].reshape(4, 2, 1, P)
        pack[l, :, PK_BS:PK_BS + 512] = np.broadcast_to(bias, (4, 2, HEAD_DIM, P)).transpose(1, 2, 0, 3).reshape(P, 512)
        for i in (1, 2, 3):
            w = a[f"hy_filt_w{i}"][l]
            for side in (0, 64):
                at = PK_W + P * (i - 1) + side
                pack[l, 0:w.shape[0], at:at + 64] = w
        pack[l, 0:64, PK_Z:PK_Z + SEQ] = z
        pack[l, 0, PK_SKIP:PK_SKIP + D_B] = a["hy_skip"][l, 0]
        w = a["hy_filt_w_out"][l].reshape(64, 2, 2, D_B)
        filt_out[l] = w.transpose(1, 2, 0, 3).reshape(2, P, D_B)

    x_t = a["x"][0].T.reshape(KT, P, SEQ).transpose(1, 0, 2)
    arrays = {
        "blocks": stream,
        "x_in": x_t,
        "params": params.transpose(0, 2, 1),
        "pack": pack,
        "filt_out": filt_out.reshape(2 * L, P, D_B),
        "skip1": a["hy_skip"][:, 1:2],
        "decay": decay,
        "identity": np.eye(P, dtype=np.float32),
    }
    arrays = {k: np.ascontiguousarray(w) for k, w in arrays.items()}
    nc = _bacc.Bacc("TRN2", target_bir_lowering=False, num_devices=1)
    args = [nc.dram_tensor(k, w.shape, F32, kind="ExternalInput").ap() for k, w in arrays.items()]
    out = nc.dram_tensor("out_t", (P, KT, SEQ), F32, kind="ExternalOutput").ap()
    build_encoder(nc, *args, out)
    r = _run(nc, [arrays], core_ids=[0])
    y = r.results[0]["out_t"]
    return np.ascontiguousarray(y.transpose(1, 0, 2).reshape(D_MODEL, SEQ).T).reshape(1, SEQ, D_MODEL)
```
